# Optimizing a Trainium2 kernel written in Bass

```python
import jax, jax.numpy as jnp
from jax import lax
import numpy as np

D_MODEL = 1024
BATCH = 1
SEQ = 256
DEPTH = 2

DN_ALPHA = (2 * DEPTH) ** 0.25
DN_BETA = (8 * DEPTH) ** -0.25
LN_EPS = 1e-5
RMS_EPS = 1e-6

CONV_CH = D_MODEL // 2
CONV_WIDTH = 31

MLA_HEADS = 8
QK_NOPE = 64
QK_ROPE = 32
V_DIM = 64
Q_LORA = D_MODEL // 4
KV_LORA = D_MODEL // 8
ROPE_THETA = 10000.0

L0_IN = 2 * CONV_CH + Q_LORA + KV_LORA + QK_ROPE
L0_MIX = CONV_CH + MLA_HEADS * V_DIM

FOX_HEADS = 16
FOX_HD = D_MODEL // FOX_HEADS
L1_IN = 3 * FOX_HEADS * FOX_HD + FOX_HEADS
L1_MIX = FOX_HEADS * FOX_HD

BLOCK_Q = 128

N_EXPERTS = 64
TOP_K = 6
N_GROUPS = 8
TOPK_GROUPS = 4
EXPERT_HID = D_MODEL // 4
SHARED_HID = EXPERT_HID
ROUTED_SCALE = 2.5

kernel_name = "hybrid_conv_mla_fox_moe_deepnorm"

def layer_norm(x, g, b):
    xf = x.astype(jnp.float32)
    mu = jnp.mean(xf, axis=-1, keepdims=True)
    var = jnp.mean(jnp.square(xf - mu), axis=-1, keepdims=True)
    return ((xf - mu) * lax.rsqrt(var + LN_EPS) * g + b).astype(x.dtype)

def rms_norm(x, g):
    xf = x.astype(jnp.float32)
    return (xf * lax.rsqrt(jnp.mean(jnp.square(xf), axis=-1, keepdims=True) + RMS_EPS) * g).astype(x.dtype)

def rope(x, cos, sin):
    x1, x2 = jnp.split(x, 2, axis=-1)
    return jnp.concatenate([x1 * cos - x2 * sin, x2 * cos + x1 * sin], axis=-1)

def causal_block_attention(q, k, v, scale, log_fcum=None):
    seq = q.shape[2]
    outs = []
    for i in range(seq // BLOCK_Q):
        q0, q1 = i * BLOCK_Q, (i + 1) * BLOCK_Q
        s = jnp.einsum('bhqd,bhkd->bhqk', q[:, :, q0:q1], k[:, :, :q1],
                       preferred_element_type=jnp.float32) * scale
        if log_fcum is not None:
            s = s + (log_fcum[:, :, q0:q1, None] - log_fcum[:, :, None, :q1])
        mask = (q0 + jnp.arange(BLOCK_Q))[:, None] >= jnp.arange(q1)[None, :]
        p = jax.nn.softmax(jnp.where(mask, s, -jnp.inf), axis=-1)
        outs.append(jnp.einsum('bhqk,bhkd->bhqd', p.astype(v.dtype), v[:, :, :q1]))
    return jnp.concatenate(outs, axis=2)

def conv_mla_mixer(x, cos, sin, w_in, b_in, conv_w, conv_b, conv_ln_g, conv_ln_b,
                   q_norm_g, w_uq, kv_norm_g, w_ukv, w_out, b_out):
    bsz, seq, _ = x.shape
    h = x @ w_in + b_in
    i1 = 2 * CONV_CH
    i2 = i1 + Q_LORA
    i3 = i2 + KV_LORA
    conv_in, q_lat, kv_lat, k_rope = h[..., :i1], h[..., i1:i2], h[..., i2:i3], h[..., i3:]

    a, g = jnp.split(conv_in, 2, axis=-1)
    u = a * jax.nn.sigmoid(g)
    u = lax.conv_general_dilated(
        u, conv_w[:, None, :].astype(u.dtype), window_strides=(1,),
        padding=[(CONV_WIDTH - 1, 0)], dimension_numbers=('NWC', 'WIO', 'NWC'),
        feature_group_count=CONV_CH) + conv_b
    u = jax.nn.silu(layer_norm(u, conv_ln_g, conv_ln_b))

    q = (rms_norm(q_lat, q_norm_g) @ w_uq).reshape(bsz, seq, MLA_HEADS, QK_NOPE + QK_ROPE)
    q = jnp.concatenate([q[..., :QK_NOPE], rope(q[..., QK_NOPE:], cos, sin)], axis=-1)
    kv = (rms_norm(kv_lat, kv_norm_g) @ w_ukv).reshape(bsz, seq, MLA_HEADS, QK_NOPE + V_DIM)
    k_pe = jnp.broadcast_to(rope(k_rope[:, :, None, :], cos, sin), (bsz, seq, MLA_HEADS, QK_ROPE))
    k = jnp.concatenate([kv[..., :QK_NOPE], k_pe], axis=-1)
    v = kv[..., QK_NOPE:]
    o = causal_block_attention(q.transpose(0, 2, 1, 3), k.transpose(0, 2, 1, 3),
                               v.transpose(0, 2, 1, 3), (QK_NOPE + QK_ROPE) ** -0.5)
    o = o.transpose(0, 2, 1, 3).reshape(bsz, seq, MLA_HEADS * V_DIM)

    return jnp.concatenate([u, o], axis=-1) @ w_out + b_out

def fox_mixer(x, w_in, b_in, w_out, b_out):
    bsz, seq, _ = x.shape
    h = x @ w_in + b_in
    qkv = h[..., :3 * L1_MIX].reshape(bsz, seq, 3, FOX_HEADS, FOX_HD).transpose(2, 0, 3, 1, 4)
    log_f = jax.nn.log_sigmoid(h[..., 3 * L1_MIX:].astype(jnp.float32))
    log_fcum = jnp.cumsum(log_f, axis=1).transpose(0, 2, 1)
    o = causal_block_attention(qkv[0], qkv[1], qkv[2], FOX_HD ** -0.5, log_fcum)
    return o.transpose(0, 2, 1, 3).reshape(bsz, seq, L1_MIX) @ w_out + b_out

def moe(x, router_w, router_bias, exp_w_gate, exp_w_up, exp_w_down, sh_w_gate, sh_w_up, sh_w_down):
    bsz, seq, d = x.shape
    t = x.reshape(-1, d)
    n_tok = t.shape[0]
    s = jax.nn.sigmoid((t @ router_w).astype(jnp.float32))
    choice = s + router_bias.astype(jnp.float32)
    grp = choice.reshape(n_tok, N_GROUPS, N_EXPERTS // N_GROUPS)
    gscore = jnp.sum(lax.top_k(grp, 2)[0], axis=-1)
    _, gidx = lax.top_k(gscore, TOPK_GROUPS)
    gmask = jnp.sum(jax.nn.one_hot(gidx, N_GROUPS, dtype=jnp.float32), axis=1) > 0
    emask = jnp.repeat(gmask, N_EXPERTS // N_GROUPS, axis=-1)
    _, eidx = lax.top_k(jnp.where(emask, choice, -jnp.inf), TOP_K)
    w = jnp.take_along_axis(s, eidx, axis=-1)
    w = w / jnp.sum(w, axis=-1, keepdims=True) * ROUTED_SCALE
    gates = jnp.sum(jax.nn.one_hot(eidx, N_EXPERTS, dtype=jnp.float32) * w[..., None], axis=1)

    def expert_step(acc, p):
        wg, wu, wd, g = p
        hid = jax.nn.silu(t @ wg) * (t @ wu)
        return acc + (hid @ wd) * g[:, None].astype(t.dtype), None

    routed, _ = lax.scan(expert_step, jnp.zeros_like(t), (exp_w_gate, exp_w_up, exp_w_down, gates.T))
    shared = (jax.nn.silu(t @ sh_w_gate) * (t @ sh_w_up)) @ sh_w_down
    return (routed + shared).reshape(bsz, seq, d)

def setup_inputs(seed: int = 0) -> dict:
    key = jax.random.key(seed)
    ks = iter(jax.random.split(key, 64))

    def nrm(shape, scale):
        return jax.random.normal(next(ks), shape, jnp.float32) * scale

    def gain(n):
        return 1.0 + nrm((n,), 0.02)

    def small(n):
        return nrm((n,), 0.02)

    def moe_params(prefix):
        return {
            prefix + "router_w": nrm((D_MODEL, N_EXPERTS), D_MODEL ** -0.5),
            prefix + "router_bias": nrm((N_EXPERTS,), 0.01),
            prefix + "exp_w_gate": nrm((N_EXPERTS, D_MODEL, EXPERT_HID), D_MODEL ** -0.5),
            prefix + "exp_w_up": nrm((N_EXPERTS, D_MODEL, EXPERT_HID), D_MODEL ** -0.5),
            prefix + "exp_w_down": nrm((N_EXPERTS, EXPERT_HID, D_MODEL), EXPERT_HID ** -0.5 * DN_BETA),
            prefix + "sh_w_gate": nrm((D_MODEL, SHARED_HID), D_MODEL ** -0.5),
            prefix + "sh_w_up": nrm((D_MODEL, SHARED_HID), D_MODEL ** -0.5),
            prefix + "sh_w_down": nrm((SHARED_HID, D_MODEL), SHARED_HID ** -0.5 * DN_BETA),
            prefix + "ln2_g": gain(D_MODEL),
            prefix + "ln2_b": small(D_MODEL),
        }

    inp = {}
    inp["x"] = nrm((BATCH, SEQ, D_MODEL), 1.0)
    offset = jax.random.randint(next(ks), (BATCH, 1), 0, 1024, dtype=jnp.int32)
    inp["positions"] = offset + jnp.arange(SEQ, dtype=jnp.int32)[None, :]
    inp["l0_w_in"] = nrm((D_MODEL, L0_IN), D_MODEL ** -0.5)
    inp["l0_b_in"] = small(L0_IN)
    inp["l0_conv_w"] = nrm((CONV_WIDTH, CONV_CH), CONV_WIDTH ** -0.5)
    inp["l0_conv_b"] = small(CONV_CH)
    inp["l0_conv_ln_g"] = gain(CONV_CH)
    inp["l0_conv_ln_b"] = small(CONV_CH)
    inp["l0_q_norm_g"] = gain(Q_LORA)
    inp["l0_w_uq"] = nrm((Q_LORA, MLA_HEADS * (QK_NOPE + QK_ROPE)), Q_LORA ** -0.5)
    inp["l0_kv_norm_g"] = gain(KV_LORA)
    inp["l0_w_ukv"] = nrm((KV_LORA, MLA_HEADS * (QK_NOPE + V_DIM)), KV_LORA ** -0.5)
    inp["l0_w_out"] = nrm((L0_MIX, D_MODEL), L0_MIX ** -0.5 * DN_BETA)
    inp["l0_b_out"] = small(D_MODEL)
    inp["l0_ln1_g"] = gain(D_MODEL)
    inp["l0_ln1_b"] = small(D_MODEL)
    inp.update(moe_params("l0_"))
    inp["l1_w_in"] = nrm((D_MODEL, L1_IN), D_MODEL ** -0.5)
    inp["l1_b_in"] = small(L1_IN)
    inp["l1_w_out"] = nrm((L1_MIX, D_MODEL), L1_MIX ** -0.5 * DN_BETA)
    inp["l1_b_out"] = small(D_MODEL)
    inp["l1_ln1_g"] = gain(D_MODEL)
    inp["l1_ln1_b"] = small(D_MODEL)
    inp.update(moe_params("l1_"))
    return inp

def reference(x, positions,
              l0_w_in, l0_b_in, l0_conv_w, l0_conv_b, l0_conv_ln_g, l0_conv_ln_b,
              l0_q_norm_g, l0_w_uq, l0_kv_norm_g, l0_w_ukv, l0_w_out, l0_b_out,
              l0_ln1_g, l0_ln1_b,
              l0_router_w, l0_router_bias, l0_exp_w_gate, l0_exp_w_up, l0_exp_w_down,
              l0_sh_w_gate, l0_sh_w_up, l0_sh_w_down, l0_ln2_g, l0_ln2_b,
              l1_w_in, l1_b_in, l1_w_out, l1_b_out, l1_ln1_g, l1_ln1_b,
              l1_router_w, l1_router_bias, l1_exp_w_gate, l1_exp_w_up, l1_exp_w_down,
              l1_sh_w_gate, l1_sh_w_up, l1_sh_w_down, l1_ln2_g, l1_ln2_b):
    inv_freq = 1.0 / (ROPE_THETA ** (jnp.arange(0, QK_ROPE, 2, dtype=jnp.float32) / QK_ROPE))
    ang = positions.astype(jnp.float32)[..., None] * inv_freq
    cos = jnp.cos(ang)[:, :, None, :].astype(x.dtype)
    sin = jnp.sin(ang)[:, :, None, :].astype(x.dtype)

    mixer_params = [
        (l0_w_in, l0_b_in, l0_conv_w, l0_conv_b, l0_conv_ln_g, l0_conv_ln_b,
         l0_q_norm_g, l0_w_uq, l0_kv_norm_g, l0_w_ukv, l0_w_out, l0_b_out),
        (l1_w_in, l1_b_in, l1_w_out, l1_b_out),
    ]
    ln1 = [(l0_ln1_g, l0_ln1_b), (l1_ln1_g, l1_ln1_b)]
    moe_p = [
        (l0_router_w, l0_router_bias, l0_exp_w_gate, l0_exp_w_up, l0_exp_w_down,
         l0_sh_w_gate, l0_sh_w_up, l0_sh_w_down),
        (l1_router_w, l1_router_bias, l1_exp_w_gate, l1_exp_w_up, l1_exp_w_down,
         l1_sh_w_gate, l1_sh_w_up, l1_sh_w_down),
    ]
    ln2 = [(l0_ln2_g, l0_ln2_b), (l1_ln2_g, l1_ln2_b)]

    for layer in range(DEPTH):
        if layer % 2 == 0:
            mix = conv_mla_mixer(x, cos, sin, *mixer_params[layer])
        else:
            mix = fox_mixer(x, *mixer_params[layer])
        x = layer_norm(DN_ALPHA * x + mix, *ln1[layer])
        x = layer_norm(DN_ALPHA * x + moe(x, *moe_p[layer]), *ln2[layer])
    return x


_drawn_inputs = setup_inputs


def setup_inputs(seed=0):
    import zlib

    import numpy as np

    out = dict(_drawn_inputs(seed))
    spreads = {}
    factors = {'l0_q_norm_g': 8.0, 'l0_kv_norm_g': 3.541, 'l1_ln2_b': 2.893, 'l0_conv_ln_b': 4.624}
    for name, (base, spread) in spreads.items():
        noise = np.random.default_rng([zlib.crc32(name.encode()), seed]).standard_normal(out[name].shape)
        drawn = base * np.exp(spread * noise) if base else spread * noise
        out[name] = __import__('jax').numpy.asarray(drawn.astype(out[name].dtype))
    for name, factor in factors.items():
        out[name] = (out[name] * factor).astype(out[name].dtype)
    return out
```

```python
from contextlib import ExitStack

import numpy as np

import concourse.bass as bass
from concourse import mybir

F32 = mybir.dt.float32
BF16 = mybir.dt.bfloat16
I32 = mybir.dt.int32
ALU = mybir.AluOpType
ACT = mybir.ActivationFunctionType
AX = mybir.AxisListType

P = 128
D = 1024
T = 256
TB = T // P
C = D // P
HALF = 512
ALPHA = 4.0 ** 0.25
LN_EPS, RMS_EPS = 1e-5, 1e-6

CONV, TAPS = 512, 31
CC = CONV // P
H0, NOPE, ROPE, VD = 8, 64, 32, 64
QK = NOPE + ROPE
QL, KVL = 256, 128
LAT = QL + KVL + ROPE
H1, HD = 16, 64

NE, TOPK, NG, TOPG, HID = 64, 6, 8, 4, 256
GS = NE // NG
SCALE = 2.5
SLOTS = 64
GE = 4
NGRP = NE // GE
GSLOT = GE * SLOTS
MAXR = T // SLOTS

NEG = -1e30
SENT = -2e30
TAKEN = 3e38
FAR = 1e6

NU = 12
UNIT = 2048
GATHER_BANKS = (4, 5)

ROUND = 1.5 * 2.0 ** 23
TWO_PI = (6.28125, 0.0019350051879882812, 3.0199159819567e-07)
FREQ = (1.0 / (np.float32(10000.0) ** (np.arange(0, ROPE, 2, dtype=np.float32) / np.float32(ROPE)))).astype(np.float32)


class Plan:

    def __init__(self):
        self.n, self.at, self.per, self.base = {}, {}, {}, {}

    def add(self, key, res):
        self.at[key] = (res, self.n.get(res, 0))
        self.n[res] = self.n.get(res, 0) + 1

    def loop(self, name, seq, times):
        self.base[name], per = dict(self.n), {}
        for key, res in seq:
            self.at[(name, key)] = (res, self.n.get(res, 0), per.get(res, 0))
            per[res] = per.get(res, 0) + 1
        self.per[name] = per
        for res, k in per.items():
            self.n[res] = self.n.get(res, 0) + k * times


def plan_banks():
    u = Plan()

    def xt(n):
        for k in range(4):
            u.add(("xt", n, k), k)

    def attention(L, heads):
        for h in range(heads + 2):
            if h < heads:
                u.add(("score", L, h), h % 3)
            if 1 <= h <= heads:
                u.add(("pt", L, h - 1), 3 + (h - 1) % 2)
            if h >= 2 and (h - 2) % 2 == 0:
                u.add(("ot", L, (h - 2) // 2), 5 + (h - 2) // 2 % 2)

    u.add("cols0", 4)
    xt(0)
    for tb in range(TB):
        u.add(("lat", tb), 4 + tb)
    for j in range(CC):
        u.add(("ag", j), [6, 7, 0, 1][j])
    for tb in range(TB):
        u.add(("latT", tb), 2 + tb)
    for tb in range(TB):
        for h in range(2):
            u.add(("q", tb, h), 4 + 2 * tb + h)
    for tb in range(TB):
        for h in range(2):
            u.add(("kv", tb, h), 2 * tb + h)
    for tb in range(TB):
        for g in range(2):
            u.add(("qT", tb, g), 4 + 2 * tb + g)
    for tb in range(TB):
        for g in range(2):
            u.add(("kT", tb, g), 2 * tb + g)
    attention(0, H0)
    for tb in range(TB):
        u.add(("urow", tb), 6 + tb)
    for tb in range(TB):
        u.add(("uT", tb), 0 + tb)
    for L in range(2):
        if L == 1:
            xt(2)
            u.add("cols1", 4)
            u.add("forget", 5)
            for n in range(8):
                u.add(("qk", n), [6, 7, 0, 1][n % 4])
            for h in range(2):
                for tb in range(TB):
                    u.add(("v", tb, h), [2, 3, 4, 5][2 * h + tb])
            attention(1, H1)
        for tb in range(TB):
            for h in range(2):
                u.add(("mix", L, tb, h), 2 * tb + h)
        xt(1 + 2 * L)
        u.add(("router", L), 4)
        for m in range(2):
            u.add(("sgu", L, m), m)
        u.add(("pos", L), 5)
        for tb in range(TB):
            for h in range(2):
                u.add(("sdn", L, tb, h), [2, 3, 6, 7][2 * tb + h])
        for c in range(C):
            u.add(("gather", L, c), GATHER_BANKS[c % 2])
        seq = [("gT", 6)]
        seq += [(("gu", pr), pr) for pr in range(GE // 2)]
        seq += [(("hT", pr), pr) for pr in range(GE // 2)]
        seq += [(("dn", pr, h), 2 + h) for pr in range(GE // 2) for h in range(2)]
        seq += [(("gather", c), GATHER_BANKS[c % 2]) for c in range(C)]
        seq += [(("scatter", n), [7, 6][n % 2]) for n in range(4)]
        u.loop(L, seq, NGRP)
    return u


def plan_units():
    u = Plan()
    for k in range(4):
        u.add(("in0", k), k)
    u.add(("lat", 0), 4)
    u.add("uq", 6)
    u.add("ukv", 7)
    for k in range(4):
        u.add(("out0", k), 8 + k)
    for k in range(3):
        u.add(("shared", 0, k), k)
    first = {0: 1, 1: 0}
    u.loop(0, [((j, k), 3 * ((first[0] + j) % 4) + k) for j in range(GE) for k in range(3)], NGRP)
    for k in range(12):
        u.add(("in1", k), (3 + k) % 12)
    for k in range(4):
        u.add(("out1", k), 3 + k)
    for k in range(3):
        u.add(("shared", 1, k), 9 + k)
    u.loop(1, [((j, k), 3 * ((first[1] + j) % 4) + k) for j in range(GE) for k in range(3)], NGRP)
    return u


class ExpertLoop:

    def __init__(self, L, banks, S, bank, r=None):
        self.L, self.plan, self.S, self.tiles, self.r = L, banks, S, bank, r
        self.i = None
        self.tag = f"{'moe' if r is None else 'more'}{L}"

    def sem(self, name):
        return self.S(f"{self.tag}_{name}")

    def count(self, per, prologue, off):
        n = prologue + off if self.i is None else self.i * per + (prologue + off)
        return n if self.r is None else self.r * (NGRP * per + prologue) + n

    def at(self, key, back=0):
        b, base, off = self.plan.at[(self.L, key)]
        per = self.plan.per[self.L][b]
        if self.r is None:
            return b, self.S(f"bank_full{b}"), self.S(f"bank_free{b}"), self.i * per + (base + off - back * per)
        pro = C // 2 if b in GATHER_BANKS else 0
        return b, self.sem(f"full{b}"), self.sem(f"free{b}"), self.count(per, pro, off - back * per)

    def at_prologue(self, c):
        b = GATHER_BANKS[c % 2]
        per = self.plan.per[self.L][b]
        return b, self.sem(f"full{b}"), self.sem(f"free{b}"), self.r * (NGRP * per + C // 2) + c // 2

    def where(self, key):
        return self.at_prologue(key[1]) if key[0] == "first" else self.at(key)

    def open(self, pe, key):
        b, _, free, n = self.where(key)
        pe.wait_ge(free, n if self.r is None else n + 1)
        return self.tiles[b]

    def made(self, ins, key):
        ins.then_inc(self.where(key)[1], 1)

    def read(self, eng, key):
        b, full, _, n = self.where(key)
        eng.wait_ge(full, n + 1)
        return self.tiles[b]

    def done(self, ins, key):
        ins.then_inc(self.where(key)[2], 1)

    def moved(self, eng, key):
        _, _, free, n = self.where(key)
        eng.wait_ge(free, n + 1 if self.r is None else n + 2)


def last_use_of_weights(j, w):
    return ("gu", j // 2) if w < 2 else ("dn", j // 2, 1)


IN_ORDER = [(j, w) for j in range(GE) for w in range(2)] + [(j, 2) for j in range(GE)]


def program(nc, I, out):
    banks, units = plan_banks(), plan_units()
    with ExitStack() as ctx:
        def sb(name, shape, dt=F32):
            return ctx.enter_context(nc.sbuf_tensor(name, shape, dt))

        sems = {}

        def S(name):
            if name not in sems:
                sems[name] = ctx.enter_context(nc.semaphore(name))
            return sems[name]

        bank = [ctx.enter_context(nc.psum_tensor(f"bank{b}", [P, HALF], F32)) for b in range(8)]
        ring = sb("ring", [P, NU * UNIT])
        xrow = sb("xrow", [P, TB, D])
        xT = sb("xT", [P, C, T])
        mixT = sb("mixT", [P, C, T])
        big = sb("big", [P, 8192])
        V = sb("V", [P, TB * D])
        par = sb("par", [P, 5, D])
        side = sb("side", [P, 3072])
        att = sb("att", [P, 1536])
        rw = sb("rw", [P, C, NE])
        wf = sb("wf", [P, C, H1])
        ident = sb("ident", [P, P])
        mask = sb("mask", [P, T])
        iota = sb("iota", [P, SLOTS])
        before = sb("before", [P, P], BF16)
        ones = sb("ones", [P, P], BF16)
        rbias = sb("rbias", [P, NE])
        cols = sb("cols", [P, 12 + CC * TAPS])
        qkcol = sb("qkcol", [P, 2, 16])
        rows1 = sb("rows1", [16, P])
        fbias = sb("fbias", [H1, 1])
        posi = sb("posi", [P, TB], I32)
        posf = sb("posf", [P, TB])
        freq = sb("freq", [P, ROPE // 2])
        turn = sb("turn", [P, 2, TB, ROPE // 2])
        st = sb("st", [P, 2, 12])
        mv = sb("mv", [P, 4])
        rstd = sb("rstd", [P, 4])
        mx = sb("mx", [P, 2, 4])
        rs = sb("rs", [P, 2, 4])
        posm = sb("posm", [P, TB, NE + GE])
        gates = sb("gates", [P, TB, NE + GE])
        gsx = sb("gsx", [P, TB, 12])
        gsr = sb("gsr", [P, TB, 12])
        top = sb("top", [P, TB, 8])
        want = sb("want", [P, TB, 8])
        pen = sb("pen", [P, TB, NG])
        half = sb("half", [P, 2])
        norm = sb("norm", [P, 4])
        rounds = sb("rounds", [P, 1], I32)

        def cut(area, at, *shape):
            n = int(np.prod(shape))
            v = area[:, at:at + n]
            if len(shape) == 2:
                return v.rearrange("p (a b) -> p a b", a=shape[0])
            if len(shape) == 3:
                return v.rearrange("p (a b c) -> p a b c", a=shape[0], b=shape[1])
            return v

        qT, kT = cut(big, 0, H1, T), cut(big, 4096, H1, T)
        qT0, kT0 = cut(big, 0, H0, T), cut(big, 2048, H0, T)
        qrow, krow = cut(big, 4096, TB, H0, QK), cut(big, 5632, TB, H0, QK)
        lat = cut(big, 7168, TB, LAT)
        V0, V1 = cut(V, 0, TB, H0 * VD), cut(V, 0, TB, D)
        cln = cut(V, 1024, 2, CONV)
        upad, urow = cut(side, 0, CC, TAPS - 1 + T), cut(side, 0, TB, CONV)
        uacc = cut(side, 1144, CC, T)
        lpar = cut(side, 2168, LAT + QL + KVL)
        vbias = cut(side, 0, D)
        latT = mixT[:, 0:3, :]
        rows0, taps0 = mixT[0:12, 3, 0:P], mixT[0:TAPS, 4:6, :].rearrange("p a b -> p (a b)")
        tapped = par[:, 3, 0:2 * T].rearrange("p (a t) -> p a t", a=2)
        ang = cut(att, 0, 2, TB, ROPE // 2)
        rt = [cut(att, 256 * k, TB, H0, ROPE // 2) for k in range(4)]
        fg = [cut(att, 256 * k, T) for k in range(5)]
        sc = [cut(att, 384 * b, 384) for b in range(2)]
        pt = [cut(att, 768 + 384 * b, 384) for b in range(2)]
        acc = mixT[:, :, :].rearrange("p c t -> p (c t)").rearrange("p (a b) -> p a b", a=TB)
        xs = [side[:, 1024 * k:1024 * k + 1024].bitcast(BF16).rearrange("p (a b) -> p a b", a=TB) for k in range(3)]
        xg = cut(big, 0, C, GSLOT)
        y = cut(big, 2048, 2, D)
        gT = cut(big, 4096, 2, T)
        hidT = [cut(big, 4608 + 256 * pr, 2, P) for pr in range(GE // 2)]
        hid = [cut(big, 5120 + 256 * pr, HID) for pr in range(GE // 2)]
        hidS, silS = cut(big, 5632, 2, T), cut(big, 6144, 2, T)
        rest = cut(big, 6656, D)
        pick = att[:, 0:GSLOT].bitcast(BF16).rearrange("p (a b) -> p a b", a=TB)
        pickg = cut(att, 256, TB, GSLOT)
        sco, cho = cut(att, 768, TB, NE), cut(att, 896, TB, NE)
        chx, exr = cut(att, 1024, TB, 72), cut(att, 1168, TB, 72)
        m8 = cut(att, 1312, TB, NG, 8)
        taken = att[:, 1440:1504].bitcast(BF16).rearrange("p (a b) -> p a b", a=TB)

        def unit(key):
            u = units.at[key][0]
            return ring[:, u * UNIT:(u + 1) * UNIT]

        def by_chunk(u):
            return u.rearrange("p (c f) -> p c f", c=C)

        def by_pair(u):
            return u.rearrange("p (m n) -> p m n", m=2)

        def bank_open(pe, key):
            b, n = banks.at[key]
            if n:
                pe.wait_ge(S(f"bank_free{b}"), n)
            return bank[b]

        def bank_made(ins, key):
            ins.then_inc(S(f"bank_full{banks.at[key][0]}"), 1)

        def bank_read(eng, key):
            b, n = banks.at[key]
            eng.wait_ge(S(f"bank_full{b}"), n + 1)
            return bank[b]

        def bank_done(ins, key):
            ins.then_inc(S(f"bank_free{banks.at[key][0]}"), 1)

        def bank_moved(eng, key):
            b, n = banks.at[key]
            eng.wait_ge(S(f"bank_free{b}"), n + 1)

        def unit_wait(pe, key):
            u, n = units.at[key]
            pe.wait_ge(S(f"unit_full{u}"), 16 * (n + 1))

        def bcast(ap, n=P):
            return ap.partition_broadcast(n)

        def loop_unit(L, j, w):
            return units.at[(L, (j, w))]

        def loop_weights(L, j, w):
            u = loop_unit(L, j, w)[0]
            a = ring[:, u * UNIT:(u + 1) * UNIT]
            return by_chunk(a) if w < 2 else by_pair(a)

        def prog_sync(sp):
            def load(key, dst, src, after=None):
                if after:
                    bank_read(sp, after)
                sp.dma_start(dst, src).then_inc(S(f"unit_full{units.at[key][0]}"), 16)

            def expert_weights(L, e, w):
                src = I[f"l{L}_exp_w_{('gate', 'up', 'down')[w]}"][bass.ds(e, 1)]
                return src.rearrange("a (p c) f -> (a p) c f", c=C) if w < 2 else \
                    src.rearrange("a (m p) n -> (a p) m n", p=P)

            for tb in range(TB):
                sp.dma_start(xrow[:, tb, :], I["x"][0, P * tb:P * tb + P, :]).then_inc(S(f"x_in{tb}"), 16)
            win = I["l0_w_in"].rearrange("(p c) n -> p c n", c=C)
            wl = ring[:, 4 * UNIT:4 * UNIT + C * LAT].rearrange("p (c n) -> p c n", c=C)
            load(("lat", 0), wl, win[:, :, 2 * CONV:])
            for k in (0, 2, 1, 3):
                load(("in0", k), by_chunk(unit(("in0", k))), win[:, :, 256 * k:256 * k + 256])
            load("uq", unit("uq")[:, 0:1536].rearrange("p (k n) -> p k n", k=2),
                 I["l0_w_uq"].rearrange("(k p) n -> p k n", p=P))
            load("ukv", unit("ukv")[:, 0:1024], I["l0_w_ukv"])
            for L in range(2):
                if L == 1:
                    win = I["l1_w_in"].rearrange("(p c) n -> p c n", c=C)
                    for j, w in IN_ORDER:
                        k = 3 * j + w
                        b, base, off = banks.at[(0, last_use_of_weights(j, w))]
                        sp.wait_ge(S(f"bank_full{b}"), base + off + 1 + (NGRP - 1) * banks.per[0][b])
                        load(("in1", k), by_chunk(unit(("in1", k))), win[:, :, 256 * k:256 * k + 256])
                wout = I[f"l{L}_w_out"].rearrange("(k j p) n -> k p j n", p=P, j=2)
                for k in range(4):
                    load((f"out{L}", k), by_pair(unit((f"out{L}", k))), wout[k],
                         after=("qk", k) if L else None)
                for w, name in enumerate(("gate", "up", "down")):
                    src = I[f"l{L}_sh_w_{name}"]
                    a = unit(("shared", L, w))
                    before_it = ("ag", 3) if L == 0 else [("qk", 6), ("qk", 7), ("v", 1, 0)][w]
                    if w < 2:
                        load(("shared", L, w), by_chunk(a), src.rearrange("(p c) f -> p c f", c=C), before_it)
                    else:
                        load(("shared", L, w), by_pair(a), src.rearrange("(m p) n -> p m n", p=P), before_it)
                mix, sgu, sdn = ("mix", L, 1, 1), ("sgu", L, 1), ("sdn", L, 1, 1)
                if L == 0:
                    held = [("ag", 3), ("lat", 1), ("lat", 1), ("q", 1, 1), ("kv", 1, 1), mix,
                            mix, mix, mix, sgu, sgu, sdn]
                else:
                    held = [("v", 1, 1)] * 3 + [mix] * 4 + [("qk", 4), ("qk", 5), sgu, sgu, sdn]
                for j in range(GE):
                    for w in range(3):
                        bank_read(sp, held[3 * j + w])
                        sp.dma_start(loop_weights(L, j, w), expert_weights(L, j, w))\
                          .then_inc(S(f"unit_full{loop_unit(L, j, w)[0]}"), 16)
                lp = ExpertLoop(L, banks, S, bank)
                with sp.Fori(1, NGRP) as i:
                    lp.i = i
                    for j, w in IN_ORDER:
                        _, full, _, n = lp.at(last_use_of_weights(j, w), back=1)
                        sp.wait_ge(full, n + 1)
                        sp.dma_start(loop_weights(L, j, w), expert_weights(L, i * GE + j, w))\
                          .then_inc(S(f"unit_full{loop_unit(L, j, w)[0]}"), 16)
                sp.wait_ge(S("rounds"), L + 1)
                more = sp.value_load(rounds[0:1, 0:1], min_val=0, max_val=MAXR - 1)
                with sp.If(more > 0):
                    with sp.Fori(0, more) as r:
                        lp = ExpertLoop(L, banks, S, bank, r)
                        sp.wait_ge(lp.sem("round"), r + 1)
                        for j in range(GE):
                            for w in range(3):
                                sp.dma_start(loop_weights(L, j, w), expert_weights(L, j, w))\
                                  .then_inc(lp.sem(f"weights{3 * j + w}"), 16)
                        with sp.Fori(1, NGRP) as i:
                            lp.i = i
                            for j, w in IN_ORDER:
                                _, full, _, n = lp.at(last_use_of_weights(j, w), back=1)
                                sp.wait_ge(full, n + 1)
                                sp.dma_start(loop_weights(L, j, w), expert_weights(L, i * GE + j, w))\
                                  .then_inc(lp.sem(f"weights{3 * j + w}"), 16)
                    sp.wait_ge(S(f"more{L}_round"), more + 1)
                    sp.sem_inc(S("rounds_seen"), 1)
                with sp.Else():
                    sp.nop()
            for tb in range(TB):
                sp.wait_ge(S("ln_done"), 6 + tb + 1)
                sp.dma_start(out[0, P * tb:P * tb + P, :], xrow[:, tb, :]).then_inc(S("stored"), 16)
            sp.wait_ge(S("stored"), 32)

        def prog_tensor(pe):
            mm, flip = nc.tensor.matmul, nc.tensor.transpose

            def xt(n):
                for tb in range(TB):
                    if n == 0:
                        pe.wait_ge(S(f"x_in{tb}"), 16)
                    else:
                        pe.wait_ge(S("ln_done"), 2 * (n - 1) + tb + 1)
                    rows = xrow[:, tb, :].rearrange("t (p c) -> t c p", c=C)
                    for g in range(2):
                        key = ("xt", n, 2 * tb + g)
                        ps = bank_open(pe, key)
                        for k in range(4):
                            ins = flip(ps[:, P * k:P * k + P], rows[:, 4 * g + k, :], ident[:])
                        bank_made(ins, key)
                for k in range(4):
                    bank_moved(pe, ("xt", n, k))

            def attention(L, heads, dk, qt, kt, v, vd):
                for h in range(heads + 2):
                    if h < heads:
                        key = ("score", L, h)
                        ps = bank_open(pe, key)
                        mm(ps[:, 0:P], qt[0:dk, h, 0:P], kt[0:dk, h, 0:P], start=True, stop=True)
                        ins = mm(ps[:, P:P + T], qt[0:dk, h, P:T], kt[0:dk, h, :], start=True, stop=True)
                        bank_made(ins, key)
                    if 1 <= h <= heads:
                        g = h - 1
                        key = ("pt", L, g)
                        ps = bank_open(pe, key)
                        pe.wait_ge(S("probs"), (H0 if L else 0) + g + 1)
                        for k in range(3):
                            ins = flip(ps[:, P * k:P * k + P], sc[g % 2][:, P * k:P * k + P], ident[:])
                        bank_made(ins, key)
                    if h >= 2:
                        g = h - 2
                        key = ("ot", L, g // 2)
                        ps = bank_open(pe, key) if g % 2 == 0 else bank[banks.at[key][0]]
                        bank_moved(pe, ("pt", L, g))
                        r = slice(64 * (g % 2), 64 * (g % 2) + 64)
                        mm(ps[r, 0:T], v[:, 0, vd * g:vd * g + vd], pt[g % 2][:, 0:T], start=True, stop=False)
                        ins = mm(ps[r, P:T], v[:, 1, vd * g:vd * g + vd], pt[g % 2][:, T:T + P], start=False, stop=True)
                        if g % 2:
                            bank_made(ins, key)

            pe.wait_ge(S("ident"), 2)
            pe.wait_ge(S("rows0"), 48)
            ps = bank_open(pe, "cols0")
            flip(ps[:, 0:12], rows0, ident[0:12, 0:12])
            for j in range(CC):
                ins = flip(ps[:, 12 + TAPS * j:12 + TAPS * j + TAPS], taps0[:, P * j:P * j + P], ident[0:TAPS, 0:TAPS])
            bank_made(ins, "cols0")
            xt(0)
            wl = ring[:, 4 * UNIT:4 * UNIT + C * LAT].rearrange("p (c n) -> p c n", c=C)
            unit_wait(pe, ("lat", 0))
            for tb in range(TB):
                ps = bank_open(pe, ("lat", tb))
                for c in range(C):
                    ins = mm(ps[:, 0:LAT], xT[:, c, P * tb:P * tb + P], wl[:, c, :], start=(c == 0), stop=(c == C - 1))
                bank_made(ins, ("lat", tb))
            for j in range(CC):
                key = ("ag", j)
                ps = bank_open(pe, key)
                for s in range(2):
                    w = by_chunk(unit(("in0", 2 * s + j // 2)))
                    unit_wait(pe, ("in0", 2 * s + j // 2))
                    for c in range(C):
                        ins = mm(ps[:, T * s:T * s + T], w[:, c, P * (j % 2):P * (j % 2) + P], xT[:, c, :],
                                 start=(c == 0), stop=(c == C - 1))
                bank_made(ins, key)
            for tb in range(TB):
                pe.wait_ge(S("lat_normed"), tb + 1)
                ps = bank_open(pe, ("latT", tb))
                for k in range(3):
                    ins = flip(ps[:, P * k:P * k + P], lat[:, tb, P * k:P * k + P], ident[:])
                bank_made(ins, ("latT", tb))
            unit_wait(pe, "uq")
            wq = unit("uq")[:, 0:1536].rearrange("p (k n) -> p k n", k=2)
            for tb in range(TB):
                bank_moved(pe, ("latT", tb))
                for h in range(2):
                    ps = bank_open(pe, ("q", tb, h))
                    for k in range(2):
                        ins = mm(ps[:, 0:384], latT[:, k, P * tb:P * tb + P], wq[:, k, 384 * h:384 * h + 384],
                                 start=(k == 0), stop=(k == 1))
                    bank_made(ins, ("q", tb, h))
            unit_wait(pe, "ukv")
            for tb in range(TB):
                for h in range(2):
                    ps = bank_open(pe, ("kv", tb, h))
                    ins = mm(ps[:], latT[:, 2, P * tb:P * tb + P], unit("ukv")[:, HALF * h:HALF * h + HALF],
                             start=True, stop=True)
                    bank_made(ins, ("kv", tb, h))
            for name, rows in (("qT", qrow), ("kT", krow)):
                pe.wait_ge(S(f"{name}_rows"), 1)
                if name == "kT":
                    for tb in range(TB):
                        for h in range(2):
                            bank_moved(pe, ("kv", tb, h))
                for tb in range(TB):
                    for g in range(2):
                        ps = bank_open(pe, (name, tb, g))
                        for k in range(4):
                            ins = flip(ps[0:QK, P * k:P * k + P], rows[:, tb, 4 * g + k, :], ident[:])
                        bank_made(ins, (name, tb, g))
            for name in ("qT", "kT"):
                for tb in range(TB):
                    for g in range(2):
                        bank_moved(pe, (name, tb, g))
            attention(0, H0, QK, qT0, kT0, V0, VD)
            pe.wait_ge(S("conv_dve"), 1)
            pe.wait_ge(S("conv_pool"), TAPS)
            for tb in range(TB):
                ps = bank_open(pe, ("urow", tb))
                for k in range(CC):
                    ins = flip(ps[:, P * k:P * k + P], uacc[:, k, P * tb:P * tb + P], ident[:])
                bank_made(ins, ("urow", tb))
            for tb in range(TB):
                pe.wait_ge(S("u_act"), tb + 1)
                ps = bank_open(pe, ("uT", tb))
                for k in range(CC):
                    ins = flip(ps[:, P * k:P * k + P], urow[:, tb, P * k:P * k + P], ident[:])
                bank_made(ins, ("uT", tb))

            for L in range(2):
                if L == 1:
                    xt(2)
                    pe.wait_ge(S("rows1"), 16)
                    ps = bank_open(pe, "cols1")
                    ins = flip(ps[:, 0:16], rows1[:], ident[0:16, 0:16])
                    bank_made(ins, "cols1")
                    pe.wait_ge(S("wf"), 16)
                    ps = bank_open(pe, "forget")
                    for c in range(C):
                        ins = mm(ps[0:H1, 0:T], wf[:, c, :], xT[:, c, :], start=(c == 0), stop=(c == C - 1))
                    bank_made(ins, "forget")
                    for n in range(8):
                        unit_wait(pe, ("in1", n))
                        w = by_chunk(unit(("in1", n)))
                        ps = bank_open(pe, ("qk", n))
                        for s in range(2):
                            for c in range(C):
                                ins = mm(ps[:, T * s:T * s + T], w[:, c, P * s:P * s + P], xT[:, c, :],
                                         start=(c == 0), stop=(c == C - 1))
                        bank_made(ins, ("qk", n))
                    for h in range(2):
                        for tb in range(TB):
                            ps = bank_open(pe, ("v", tb, h))
                            for s in range(2):
                                unit_wait(pe, ("in1", 8 + 2 * h + s))
                                w = by_chunk(unit(("in1", 8 + 2 * h + s)))
                                for c in range(C):
                                    ins = mm(ps[:, 256 * s:256 * s + 256], xT[:, c, P * tb:P * tb + P], w[:, c, :],
                                             start=(c == 0), stop=(c == C - 1))
                            bank_made(ins, ("v", tb, h))
                    for n in range(8):
                        bank_moved(pe, ("qk", n))
                    pe.wait_ge(S("decay_rows"), 32)
                    for h in range(2):
                        for tb in range(TB):
                            bank_moved(pe, ("v", tb, h))
                    attention(1, H1, HD + 2, qT, kT, V1, HD)
                if L == 0:
                    for tb in range(TB):
                        bank_moved(pe, ("uT", tb))
                for g in range((H1 if L else H0) // 2):
                    bank_moved(pe, ("ot", L, g))
                for tb in range(TB):
                    for h in range(2):
                        ps = bank_open(pe, ("mix", L, tb, h))
                        for k in range(4):
                            unit_wait(pe, (f"out{L}", k))
                            w = by_pair(unit((f"out{L}", k)))
                            for j in range(2):
                                ins = mm(ps[:], mixT[:, 2 * k + j, P * tb:P * tb + P], w[:, j, HALF * h:HALF * h + HALF],
                                         start=(k + j == 0), stop=(k == 3 and j == 1))
                        bank_made(ins, ("mix", L, tb, h))
                xt(1 + 2 * L)
                pe.wait_ge(S("router_w"), 32 * (L + 1))
                ps = bank_open(pe, ("router", L))
                for tb in range(TB):
                    for c in range(C):
                        ins = mm(ps[:, NE * tb:NE * tb + NE], xT[:, c, P * tb:P * tb + P], rw[:, c, :],
                                 start=(c == 0), stop=(c == C - 1))
                bank_made(ins, ("router", L))
                for m in range(2):
                    ps = bank_open(pe, ("sgu", L, m))
                    for s in range(2):
                        unit_wait(pe, ("shared", L, s))
                        w = by_chunk(unit(("shared", L, s)))
                        for c in range(C):
                            ins = mm(ps[:, T * s:T * s + T], w[:, c, P * m:P * m + P], xT[:, c, :],
                                     start=(c == 0), stop=(c == C - 1))
                    bank_made(ins, ("sgu", L, m))
                pe.wait_ge(S("taken"), L + 1)
                pe.wait_ge(S("consts"), 6)
                ps = bank_open(pe, ("pos", L))
                mm(ps[:, 0:NE], before[:], taken[:, 0, :], start=True, stop=True)
                mm(ps[:, NE:2 * NE], ones[:], taken[:, 0, :], start=True, stop=False)
                mm(ps[:, NE:2 * NE], before[:], taken[:, 1, :], start=False, stop=True)
                mm(ps[:, 2 * NE:3 * NE], ones[:], taken[:, 0, :], start=True, stop=False)
                ins = mm(ps[:, 2 * NE:3 * NE], ones[:], taken[:, 1, :], start=False, stop=True)
                bank_made(ins, ("pos", L))
                unit_wait(pe, ("shared", L, 2))
                dw = by_pair(unit(("shared", L, 2)))
                for m in range(2):
                    bank_moved(pe, ("sgu", L, m))
                for tb in range(TB):
                    for h in range(2):
                        ps = bank_open(pe, ("sdn", L, tb, h))
                        for m in range(2):
                            ins = mm(ps[:], hidS[:, m, P * tb:P * tb + P], dw[:, m, HALF * h:HALF * h + HALF],
                                     start=(m == 0), stop=(m == 1))
                        bank_made(ins, ("sdn", L, tb, h))

                def gather(c, ps):
                    for tb in range(TB):
                        for k in range(3):
                            part = xs[k][:, tb, :].rearrange("t (p c) -> t c p", c=C)
                            ins = mm(ps[:, 0:GSLOT], part[:, c, :], pick[:, tb, :],
                                     start=(tb + k == 0), stop=(tb == 1 and k == 2))
                    return ins

                def weights_landed(lp, j, w):
                    if lp.r is None:
                        u, base, _ = loop_unit(L, j, w)
                        pe.wait_ge(S(f"unit_full{u}"), lp.i * 16 + 16 * (base + 1))
                    else:
                        pe.wait_ge(lp.sem(f"weights{3 * j + w}"), lp.r * (16 * NGRP) + lp.i * 16 + 16)

                def gate_up(lp, pr):
                    ps = lp.open(pe, ("gu", pr))
                    for q in range(2):
                        for w in range(2):
                            weights_landed(lp, 2 * pr + q, w)
                    for c in range(C):
                        for q in range(2):
                            j = 2 * pr + q
                            u = loop_unit(L, j, 0)[0]
                            both = ring[:, u * UNIT:(u + 2) * UNIT].rearrange("p (w c f) -> p c w f", w=2, c=C)
                            ins = mm(ps[SLOTS * q:SLOTS * q + SLOTS, :], xg[:, c, SLOTS * j:SLOTS * j + SLOTS],
                                     both[:, c], start=(c == 0), stop=(c == C - 1))
                    lp.made(ins, ("gu", pr))

                def flip_hidden(lp, pr):
                    ps = lp.open(pe, ("hT", pr))
                    for m in range(2):
                        ins = flip(ps[:, P * m:P * m + P], hid[pr][:, P * m:P * m + P], ident[:])
                    lp.made(ins, ("hT", pr))

                def down(lp, pr):
                    lp.moved(pe, ("hT", pr))
                    for q in range(2):
                        weights_landed(lp, 2 * pr + q, 2)
                    for h in range(2):
                        ps = lp.open(pe, ("dn", pr, h))
                        for m in range(2):
                            for q in range(2):
                                wt = loop_weights(L, 2 * pr + q, 2)
                                ins = mm(ps[SLOTS * q:SLOTS * q + SLOTS, :], hidT[pr][:, m, SLOTS * q:SLOTS * q + SLOTS],
                                         wt[:, m, HALF * h:HALF * h + HALF], start=(m == 0), stop=(m == 1))
                        lp.made(ins, ("dn", pr, h))

                def gathers(lp, cs):
                    for c in cs:
                        lp.made(gather(c, lp.open(pe, ("gather", c))), ("gather", c))

                def group(lp):
                    pe.wait_ge(lp.sem("pick"), lp.count(2, 2, 0))
                    ps = lp.open(pe, "gT")
                    for pr in range(2):
                        for tb in range(TB):
                            ins = flip(ps[:, T * pr + P * tb:T * pr + P * tb + P], pickg[:, tb, P * pr:P * pr + P], ident[:])
                    lp.made(ins, "gT")
                    for b in GATHER_BANKS:
                        per = banks.per[L][b]
                        if lp.r is None:
                            pe.wait_ge(S(f"bank_free{b}"), lp.i * per + banks.base[L][b])
                        else:
                            pe.wait_ge(lp.sem(f"free{b}"), lp.count(per, C // 2, 0) + 1)
                    gate_up(lp, 0)
                    gate_up(lp, 1)
                    flip_hidden(lp, 0)
                    pe.wait_ge(lp.sem("pick"), lp.count(2, 2, 1))
                    gathers(lp, (0, 1))
                    down(lp, 0)
                    flip_hidden(lp, 1)
                    gathers(lp, (2, 3, 4, 5))
                    down(lp, 1)
                    gathers(lp, (6, 7))
                    lp.moved(pe, "gT")
                    for h in range(2):
                        lp.moved(pe, ("dn", 1, h))
                    for n in range(4):
                        tb, h = divmod(n, 2)
                        ps = lp.open(pe, ("scatter", n))
                        for pr in range(2):
                            ins = mm(ps[:], gT[:, pr, P * tb:P * tb + P], y[:, pr, HALF * h:HALF * h + HALF],
                                     start=(pr == 0), stop=(pr == 1))
                        lp.made(ins, ("scatter", n))

                lp = ExpertLoop(L, banks, S, bank)
                pe.wait_ge(S("xs"), L + 1)
                pe.wait_ge(lp.sem("pick"), 1)
                for c in range(C):
                    bank_made(gather(c, bank_open(pe, ("gather", L, c))), ("gather", L, c))
                with pe.Fori(0, NGRP) as i:
                    lp.i = i
                    group(lp)
                pe.wait_ge(S("rounds"), L + 1)
                more = pe.value_load(rounds[0:1, 0:1], min_val=0, max_val=MAXR - 1)
                with pe.If(more > 0):
                    for b in range(8):
                        pe.wait_ge(S(f"bank_free{b}"), banks.base[L][b] + NGRP * banks.per[L][b])
                        pe.sem_inc(S(f"more{L}_free{b}"), 1)
                    with pe.Fori(0, more) as r:
                        lp = ExpertLoop(L, banks, S, bank, r)
                        pe.wait_ge(lp.sem("pick"), lp.count(2, 2, -1))
                        for c in range(C):
                            lp.made(gather(c, lp.open(pe, ("first", c))), ("first", c))
                        with pe.Fori(0, NGRP) as i:
                            lp.i = i
                            group(lp)
                    for b in range(8):
                        n = NGRP * banks.per[L][b] + (C // 2 if b in GATHER_BANKS else 0)
                        pe.wait_ge(S(f"more{L}_free{b}"), more * n + 1)
                    pe.nop()
                with pe.Else():
                    pe.nop()

        def prog_scalar(act):
            fn = nc.scalar.activation

            def xt(n):
                for k in (0, 2):
                    ps = bank_read(act, ("xt", n, k))
                    tb = k // 2
                    ins = fn(xT[:, 0:4, P * tb:P * tb + P], ps[:].rearrange("p (c t) -> p c t", c=4), ACT.Copy)
                    bank_done(ins, ("xt", n, k))

            def attention(L, heads, first):
                for h in range(heads + 2):
                    if h < heads:
                        s = sc[h % 2]
                        act.wait_ge(S("softmax"), first + h + 1)
                        fn(s[:, 0:P], s[:, 0:P], ACT.Exp, bias=mx[:, h % 2, 2:3], accum_out=rs[:, h % 2, 0:1])
                        fn(s[:, P:P + T], s[:, P:P + T], ACT.Exp, bias=mx[:, h % 2, 3:4],
                           accum_out=rs[:, h % 2, 1:2]).then_inc(S("exps"), 1)
                    if 1 <= h <= heads:
                        g = h - 1
                        ps = bank_read(act, ("pt", L, g))
                        ins = fn(pt[g % 2], ps[:, 0:384], ACT.Copy)
                        bank_done(ins, ("pt", L, g))
                    if h >= 2 and h % 2:
                        g = (h - 3) // 2
                        ps = bank_read(act, ("ot", L, g))
                        ins = fn(mixT[:, (4 if L == 0 else 0) + g, :], ps[:, 0:T], ACT.Copy)
                        bank_done(ins, ("ot", L, g))

            act.dma_start(rows0[0:8], I["l0_b_in"][0:1024].rearrange("(a b) -> a b", a=8)).then_inc(S("rows0"), 16)
            act.dma_start(mixT[8:12, 3, 0:P], I["l0_conv_b"].rearrange("(a b) -> a b", a=4)).then_inc(S("rows0"), 16)
            act.dma_start(taps0, I["l0_conv_w"]).then_inc(S("rows0"), 16)
            act.dma_start(lpar[:, 0:LAT], bcast(I["l0_b_in"][1024:1440])).then_inc(S("lpar"), 16)
            act.dma_start(lpar[:, LAT:LAT + QL], bcast(I["l0_q_norm_g"])).then_inc(S("lpar"), 16)
            act.dma_start(lpar[:, LAT + QL:], bcast(I["l0_kv_norm_g"])).then_inc(S("lpar"), 16)
            with nc.allow_non_contiguous_dma(reason="256 positions, one to a partition"):
                act.dma_start(posi[:], I["positions"][0].rearrange("(a p) -> p a", p=P)).then_inc(S("positions"), 16)
                act.dma_start(fbias[:], I["l1_b_in"][3 * D:].rearrange("(p a) -> p a", a=1)).then_inc(S("fbias"), 16)
            act.dma_start(cln[:, 0, :], bcast(I["l0_conv_ln_g"])).then_inc(S("cln"), 16)
            act.dma_start(cln[:, 1, :], bcast(I["l0_conv_ln_b"])).then_inc(S("cln"), 16)
            act.dma_start(rows1[:], I["l1_b_in"][0:2048].rearrange("(a b) -> a b", a=16)).then_inc(S("rows1"), 16)
            ps = bank_read(act, "cols0")
            bank_done(fn(cols[:], ps[:, 0:12 + CC * TAPS], ACT.Copy), "cols0")
            xt(0)
            bank_moved(act, "cols0")
            for j in range(CC):
                ps = bank_read(act, ("ag", j))
                fn(uacc[:, j, :], ps[:, T:2 * T], ACT.Sigmoid, bias=cols[:, 4 + j:5 + j]).then_inc(S("gate"), 1)
            for tb in range(TB):
                ps = bank_read(act, ("latT", tb))
                ins = fn(latT[:, :, P * tb:P * tb + P], ps[:, 0:384].rearrange("p (c t) -> p c t", c=3), ACT.Copy)
                bank_done(ins, ("latT", tb))
            act.wait_ge(S("angles"), 1)
            fn(turn[:], ang, ACT.Sin).then_inc(S("turn"), 1)
            for tb in range(TB):
                for h in range(2):
                    ps = bank_read(act, ("q", tb, h))
                    ins = fn(qrow[:, tb, 4 * h:4 * h + 4, :], ps[:, 0:384].rearrange("p (h d) -> p h d", h=4), ACT.Copy)
                    bank_done(ins, ("q", tb, h))
            for tb in range(TB):
                for h in range(2):
                    ps = bank_read(act, ("kv", tb, h))[:].rearrange("p (h d) -> p h d", h=4)
                    fn(krow[:, tb, 4 * h:4 * h + 4, 0:NOPE], ps[:, :, 0:NOPE], ACT.Copy)
                    ins = fn(V0[:, tb, 256 * h:256 * h + 256].rearrange("p (h d) -> p h d", h=4), ps[:, :, NOPE:], ACT.Copy)
                    bank_done(ins, ("kv", tb, h))
            for tb in range(TB):
                for g in range(2):
                    ps = bank_read(act, ("qT", tb, g))
                    ins = fn(qT0[0:QK, 4 * g:4 * g + 4, P * tb:P * tb + P],
                             ps[0:QK, :].rearrange("p (h t) -> p h t", h=4), ACT.Copy)
                    bank_done(ins, ("qT", tb, g))
            attention(0, H0, 0)
            for tb in range(TB):
                act.wait_ge(S("u_normed"), tb + 1)
                fn(urow[:, tb, :], urow[:, tb, :], ACT.Silu).then_inc(S("u_act"), 1)
            for tb in range(TB):
                ps = bank_read(act, ("uT", tb))
                ins = fn(mixT[:, 0:CC, P * tb:P * tb + P], ps[:].rearrange("p (c t) -> p c t", c=CC), ACT.Copy)
                bank_done(ins, ("uT", tb))
            for L in range(2):
                if L == 1:
                    xt(2)
                    act.wait_ge(S("forget"), 1)
                    fn(fg[1][0:H1], fg[1][0:H1], ACT.Exp).then_inc(S("forget_act"), 1)
                    act.wait_ge(S("forget"), 2)
                    fn(fg[1][0:H1], fg[1][0:H1], ACT.Ln).then_inc(S("forget_act"), 1)
                    act.wait_ge(S("qkcol"), 1)
                    for n in range(0, 8, 2):
                        ps = bank_read(act, ("qk", n))
                        for s in range(2):
                            for o in range(2):
                                head = 4 * (n % 4) + 2 * s + o
                                r = slice(64 * o, 64 * o + 64)
                                ins = fn((qT if n < 4 else kT)[0:HD, head, :], ps[r, T * s:T * s + T], ACT.Identity,
                                         bias=qkcol[r, 1, 2 * n + s:2 * n + s + 1], scale=HD ** -0.5 if n < 4 else 1.0)
                        bank_done(ins, ("qk", n))
                    attention(1, H1, H0)
                xt(1 + 2 * L)
                ps = bank_read(act, ("router", L))
                bank_done(fn(sco, ps[:, 0:TB * NE].rearrange("p (a e) -> p a e", a=TB), ACT.Sigmoid), ("router", L))
                for m in range(2):
                    ps = bank_read(act, ("sgu", L, m))
                    fn(silS[:, m, :], ps[:, 0:T], ACT.Silu).then_inc(S("silS"), 1)
                for tb in range(TB):
                    for h in range(2):
                        ps = bank_read(act, ("sdn", L, tb, h))
                        bank_done(fn(acc[:, tb, HALF * h:HALF * h + HALF], ps[:], ACT.Copy), ("sdn", L, tb, h))

                def gathered(read, done, key):
                    c = key[-1]
                    ps = read(act, key)
                    done(fn(xg[:, c, :], ps[:, 0:GSLOT], ACT.Copy), key)

                def group(lp):
                    ps = lp.read(act, "gT")
                    lp.done(fn(gT, ps[:].rearrange("p (a t) -> p a t", a=2), ACT.Copy), "gT")

                    def silu(pr):
                        ps = lp.read(act, ("gu", pr))
                        fn(hid[pr], ps[:, 0:HID], ACT.Silu).then_inc(lp.sem("silu"), 1)

                    def flipped(pr):
                        ps = lp.read(act, ("hT", pr))
                        lp.done(fn(hidT[pr], ps[:, 0:2 * P].rearrange("p (m s) -> p m s", m=2), ACT.Copy), ("hT", pr))

                    def rows(pr):
                        ps = lp.read(act, ("dn", pr, 0))
                        lp.done(fn(y[:, pr, 0:HALF], ps[:], ACT.Copy), ("dn", pr, 0))

                    silu(0)
                    silu(1)
                    flipped(0)
                    gathered(lp.read, lp.done, ("gather", 0))
                    rows(0)
                    flipped(1)
                    gathered(lp.read, lp.done, ("gather", 2))
                    gathered(lp.read, lp.done, ("gather", 4))
                    rows(1)
                    gathered(lp.read, lp.done, ("gather", 6))

                for c in range(0, C, 2):
                    gathered(bank_read, bank_done, ("gather", L, c))
                lp = ExpertLoop(L, banks, S, bank)
                with act.Fori(0, NGRP) as i:
                    lp.i = i
                    group(lp)
                act.wait_ge(S("rounds"), L + 1)
                more = act.value_load(rounds[0:1, 0:1], min_val=0, max_val=MAXR - 1)
                with act.If(more > 0):
                    with act.Fori(0, more) as r:
                        lp = ExpertLoop(L, banks, S, bank, r)
                        for c in range(0, C, 2):
                            gathered(lp.read, lp.done, ("first", c))
                        with act.Fori(0, NGRP) as i:
                            lp.i = i
                            group(lp)
                    act.nop()
                with act.Else():
                    act.nop()

        def prog_vector(dve):
            v = nc.vector
            steps, roots = [0], [0]

            def link(ins):
                steps[0] += 1
                ins.then_inc(S("dve_step"), 1)
                dve.wait_ge(S("dve_step"), steps[0])

            def xt(n):
                for k in (1, 3):
                    ps = bank_read(dve, ("xt", n, k))
                    tb = k // 2
                    ins = v.tensor_copy(xT[:, 4:8, P * tb:P * tb + P], ps[:].rearrange("p (c t) -> p c t", c=4))
                    bank_done(ins, ("xt", n, k))

            def inv_sqrt(dst, src, scale, eps):
                roots[0] += 1
                v.tensor_scalar(dst, src, scale, eps, ALU.mult, ALU.add).then_inc(S("variance"), 1)
                dve.wait_ge(S("inv_std"), roots[0])

            def layer_norm(tb, n, g, b):
                row = xrow[:, tb, :]
                for h in range(2):
                    ins = v.bn_stats(st[:, tb, 6 * h:6 * h + 6], row[:, HALF * h:HALF * h + HALF])
                link(ins)
                link(v.bn_aggr(mv[:, 2 * tb:2 * tb + 2], st[:, tb, :]))
                inv_sqrt(rstd[:, tb:tb + 1], mv[:, 2 * tb + 1:2 * tb + 2], 1.0, LN_EPS)
                link(v.tensor_scalar(row, row, mv[:, 2 * tb:2 * tb + 1], rstd[:, tb:tb + 1], ALU.subtract, ALU.mult))
                link(v.tensor_tensor(row, row, par[:, g, :], ALU.mult))
                v.tensor_tensor(row, row, par[:, b, :], ALU.add).then_inc(S("ln_done"), 1)

            def attention(L, heads, first, scale):
                for h in range(heads + 1):
                    if h < heads:
                        ps = bank_read(dve, ("score", L, h))
                        s = sc[h % 2]
                        if h >= 2:
                            bank_read(dve, ("pt", L, h - 2))
                        v.tensor_tensor_reduce(s[:, 0:P], ps[:, 0:P], mask[:, P:T], scale, NEG, ALU.add, ALU.max,
                                               mx[:, h % 2, 0:1])
                        ins = v.tensor_tensor_reduce(s[:, P:P + T], ps[:, P:P + T], mask[:], scale, NEG, ALU.add,
                                                     ALU.max, mx[:, h % 2, 1:2])
                        bank_done(ins, ("score", L, h))
                        bank_moved(dve, ("score", L, h))
                        v.tensor_scalar(mx[:, h % 2, 2:4], mx[:, h % 2, 0:2], -1.0, None, ALU.mult)\
                         .then_inc(S("softmax"), 1)
                    if h >= 1:
                        g = h - 1
                        dve.wait_ge(S("exps"), first + g + 1)
                        link(v.reciprocal(rs[:, g % 2, 2:4], rs[:, g % 2, 0:2]))
                        s = sc[g % 2]
                        v.tensor_scalar(s[:, 0:P], s[:, 0:P], rs[:, g % 2, 2:3], None, ALU.mult)
                        v.tensor_scalar(s[:, P:P + T], s[:, P:P + T], rs[:, g % 2, 3:4], None, ALU.mult)\
                         .then_inc(S("probs"), 1)

            def conv(j):
                ps = bank_read(dve, ("ag", j))
                dve.wait_ge(S("gate"), j + 1)
                ins = v.scalar_tensor_tensor(upad[:, j, TAPS - 1:], ps[:, 0:T], cols[:, j:j + 1], uacc[:, j, :],
                                             ALU.add, ALU.mult)
                bank_done(ins, ("ag", j))
                if j == CC - 1:
                    return
                bank_moved(dve, ("ag", j))
                w = 12 + TAPS * j
                v.tensor_scalar(uacc[:, j, :], upad[:, j, 0:T], cols[:, w:w + 1], cols[:, 8 + j:9 + j],
                                ALU.mult, ALU.add).then_inc(S("tap"), 1)
                with dve.Fori(1, TAPS) as k:
                    dve.wait_ge(S("tap"), k + j * TAPS)
                    v.scalar_tensor_tensor(uacc[:, j, :], upad[:, j, bass.ds(k, T)], cols[:, bass.ds(k + w, 1)],
                                           uacc[:, j, :], ALU.mult, ALU.add).then_inc(S("tap"), 1)

            dve.wait_ge(S("freq"), 1)
            v.memset(upad[:, :, 0:TAPS - 1], 0.0).then_inc(S("pad"), 1)
            dve.wait_ge(S("positions"), 16)
            link(v.tensor_copy(posf[:], posi[:]))
            a = ang[:, 0]
            turns = cut(att, 128, TB, ROPE // 2)
            for tb in range(TB):
                ins = v.tensor_scalar(a[:, tb, :], freq[:], posf[:, tb:tb + 1], None, ALU.mult)
            link(ins)
            for s in (1, 0):
                link(v.tensor_scalar(turns, a, 1.0 / (2 * np.pi), 0.25 * s, ALU.mult, ALU.add))
                link(v.tensor_scalar(turns, turns, ROUND, None, ALU.add))
                link(v.tensor_scalar(turns, turns, ROUND, None, ALU.subtract))
                for n, part in enumerate(TWO_PI):
                    link(v.scalar_tensor_tensor(ang[:, s], turns, -part, a if n == 0 else ang[:, s], ALU.mult, ALU.add))
                link(v.tensor_scalar(ang[:, s], ang[:, s], 0.5 * np.pi * s, float(np.pi), ALU.add, ALU.min))
                ins = v.tensor_scalar(ang[:, s], ang[:, s], -float(np.pi), None, ALU.max)
                if s:
                    link(ins)
                else:
                    ins.then_inc(S("angles"), 1)
            xt(0)
            dve.wait_ge(S("lpar"), 48)
            for tb in range(TB):
                ps = bank_read(dve, ("lat", tb))
                ins = v.tensor_tensor(lat[:, tb, :], ps[:, 0:LAT], lpar[:, 0:LAT], ALU.add)
                bank_done(ins, ("lat", tb))
                bank_moved(dve, ("lat", tb))
                parts = ((0, QL), (QL, KVL))
                for k, (at, n) in enumerate(parts):
                    x = lat[:, tb, at:at + n]
                    ins = v.tensor_tensor_reduce(cut(att, 1024 + 256 * k, n), x, x, 1.0 / n, 0.0, ALU.mult, ALU.add,
                                                 norm[:, 2 * tb + k:2 * tb + k + 1])
                link(ins)
                both = norm[:, 2 * tb:2 * tb + 2]
                inv_sqrt(both, both, 1.0, RMS_EPS)
                for k, (at, n) in enumerate(parts):
                    x = lat[:, tb, at:at + n]
                    ins = v.scalar_tensor_tensor(x, x, norm[:, 2 * tb + k:2 * tb + k + 1],
                                                 lpar[:, LAT + at:LAT + at + n], ALU.mult, ALU.mult)
                ins.then_inc(S("lat_normed"), 1)
            conv(0)
            conv(1)
            conv(2)
            conv(3)
            dve.wait_ge(S("tap"), TAPS * (CC - 1))
            v.memset(st[:], 0.0).then_inc(S("conv_dve"), 1)
            dve.wait_ge(S("turn"), 1)

            def rotate(x1, x2, o1, o2, heads):
                shape = [P, TB, heads, ROPE // 2]
                s, c = (turn[:, k].unsqueeze(2).to_broadcast(shape) for k in range(2))
                t = [a[:, :, 0:heads, :] for a in rt]
                v.tensor_tensor(t[0], x1, c, ALU.mult)
                v.tensor_tensor(t[1], x2, s, ALU.mult)
                v.tensor_tensor(t[2], x2, c, ALU.mult)
                link(v.tensor_tensor(t[3], x1, s, ALU.mult))
                v.tensor_tensor(o1, t[0], t[1], ALU.subtract)
                return v.tensor_tensor(o2, t[2], t[3], ALU.add)

            kr = lat[:, :, QL + KVL:].unsqueeze(2)
            link(rotate(kr[:, :, :, 0:16], kr[:, :, :, 16:32], kr[:, :, :, 0:16], kr[:, :, :, 16:32], 1))
            for tb in range(TB):
                ins = v.tensor_copy(krow[:, tb, :, NOPE:], lat[:, tb:tb + 1, QL + KVL:].to_broadcast([P, H0, ROPE]))
            link(ins)
            for tb in range(TB):
                for h in range(2):
                    bank_moved(dve, ("q", tb, h))
            qa, qb = qrow[:, :, :, NOPE:NOPE + 16], qrow[:, :, :, NOPE + 16:]
            rotate(qa, qb, qa, qb, H0).then_inc(S("qT_rows"), 1)
            v.memset(rs[:], 0.0).then_inc(S("kT_rows"), 1)
            for tb in range(TB):
                for g in range(2):
                    ps = bank_read(dve, ("kT", tb, g))
                    ins = v.tensor_copy(kT0[0:QK, 4 * g:4 * g + 4, P * tb:P * tb + P],
                                        ps[0:QK, :].rearrange("p (h t) -> p h t", h=4))
                    bank_done(ins, ("kT", tb, g))
            attention(0, H0, 0, QK ** -0.5)
            dve.wait_ge(S("cln"), 32)
            for tb in range(TB):
                ps = bank_read(dve, ("urow", tb))
                link(v.bn_stats(st[:, tb, 0:6], ps[:]))
                link(v.bn_aggr(mv[:, 2 * tb:2 * tb + 2], st[:, tb, 0:6]))
                inv_sqrt(rstd[:, tb:tb + 1], mv[:, 2 * tb + 1:2 * tb + 2], 1.0, LN_EPS)
                ins = v.tensor_scalar(urow[:, tb, :], ps[:], mv[:, 2 * tb:2 * tb + 1], rstd[:, tb:tb + 1],
                                      ALU.subtract, ALU.mult)
                bank_done(ins, ("urow", tb))
                bank_moved(dve, ("urow", tb))
                link(v.tensor_tensor(urow[:, tb, :], urow[:, tb, :], cln[:, 0, :], ALU.mult))
                v.tensor_tensor(urow[:, tb, :], urow[:, tb, :], cln[:, 1, :], ALU.add).then_inc(S("u_normed"), 1)

            for L in range(2):
                if L == 1:
                    xt(2)
                    ps = bank_read(dve, "cols1")
                    bank_done(v.tensor_copy(qkcol[:, 0, :], ps[:, 0:16]), "cols1")
                    bank_moved(dve, "cols1")
                    v.tensor_copy(qkcol[:, 1, 8:16], qkcol[:, 0, 8:16])
                    v.tensor_scalar(qkcol[:, 1, 0:8], qkcol[:, 0, 0:8], HD ** -0.5, None, ALU.mult).then_inc(S("qkcol"), 1)
                    z, e, one, F, nF = (f[0:H1] for f in fg)
                    ps = bank_read(dve, "forget")
                    dve.wait_ge(S("fbias"), 16)
                    ins = v.tensor_scalar(z, ps[0:H1, 0:T], fbias[:], None, ALU.add)
                    bank_done(ins, "forget")
                    bank_moved(dve, "forget")
                    link(v.memset(one, 1.0))
                    v.scalar_tensor_tensor(e, z, -1.0, z, ALU.mult, ALU.min).then_inc(S("forget"), 1)
                    dve.wait_ge(S("forget_act"), 1)
                    v.tensor_scalar(e, e, 1.0, None, ALU.add).then_inc(S("forget"), 1)
                    dve.wait_ge(S("forget_act"), 2)
                    link(v.scalar_tensor_tensor(z, z, 0.0, e, ALU.min, ALU.subtract))
                    link(v.tensor_tensor_scan(F, one, z, 0.0, ALU.mult, ALU.add))
                    v.tensor_scalar(nF, F, -1.0, None, ALU.mult).then_inc(S("decay"), 1)
                    for n in range(1, 8, 2):
                        ps = bank_read(dve, ("qk", n))
                        for s in range(2):
                            for o in range(2):
                                head = 4 * (n % 4) + 2 * s + o
                                r = slice(64 * o, 64 * o + 64)
                                ins = v.tensor_scalar((qT if n < 4 else kT)[0:HD, head, :], ps[r, T * s:T * s + T],
                                                      qkcol[r, 0, 2 * n + s:2 * n + s + 1], HD ** -0.5 if n < 4 else 1.0,
                                                      ALU.add, ALU.mult)
                        bank_done(ins, ("qk", n))
                    dve.wait_ge(S("vbias"), 16)
                    for h in range(2):
                        for tb in range(TB):
                            ps = bank_read(dve, ("v", tb, h))
                            ins = v.tensor_tensor(V1[:, tb, HALF * h:HALF * h + HALF], ps[:],
                                                  vbias[:, HALF * h:HALF * h + HALF], ALU.add)
                            bank_done(ins, ("v", tb, h))
                    dve.wait_ge(S("decay_rows"), 32)
                    attention(1, H1, H0, 1.0)
                dve.wait_ge(S("scaled"), 4 * L + 4)
                dve.wait_ge(S(f"par{L}"), 48)
                for tb in range(TB):
                    for h in range(2):
                        ps = bank_read(dve, ("mix", L, tb, h))
                        part = xrow[:, tb, HALF * h:HALF * h + HALF]
                        bank_done(v.tensor_tensor(part, part, ps[:], ALU.add), ("mix", L, tb, h))
                    for h in range(2):
                        bank_moved(dve, ("mix", L, tb, h))
                    layer_norm(tb, 2 * L, 1, 2)
                xt(1 + 2 * L)
                bank_moved(dve, ("router", L))
                dve.wait_ge(S("router_w"), 32 * (L + 1))
                v.memset(gsx[:], SENT)
                v.memset(chx[:, :, NE:], SENT)
                v.memset(want[:], SENT)
                link(v.tensor_tensor(cho, sco, rbias[:].unsqueeze(1).to_broadcast([P, TB, NE]), ALU.add))
                for tb in range(TB):
                    for g in range(NG):
                        ins = v.max(m8[:, tb, g, :], cho[:, tb, GS * g:GS * g + GS])
                link(ins)
                link(v.tensor_tensor(gsx[:, :, 0:NG], m8[:, :, :, 0], m8[:, :, :, 1], ALU.add))
                for tb in range(TB):
                    ins = v.max(top[:, tb, :], gsx[:, tb, 0:NG])
                link(ins)
                link(v.tensor_copy(want[:, :, 0:TOPG], top[:, :, 0:TOPG]))
                for tb in range(TB):
                    ins = v.match_replace(gsr[:, tb, :], want[:, tb, :], gsx[:, tb, :], TAKEN)
                link(ins)
                link(v.tensor_scalar(pen[:], gsr[:, :, 0:NG], TAKEN, NEG, ALU.not_equal, ALU.mult))
                link(v.tensor_tensor(chx[:, :, 0:NE].rearrange("p a (g k) -> p a g k", g=NG),
                                     cho.rearrange("p a (g k) -> p a g k", g=NG),
                                     pen[:].unsqueeze(3).to_broadcast([P, TB, NG, GS]), ALU.add))
                for tb in range(TB):
                    ins = v.max(top[:, tb, :], chx[:, tb, 0:NE])
                link(ins)
                link(v.tensor_copy(want[:, :, 0:TOPK], top[:, :, 0:TOPK]))
                for tb in range(TB):
                    ins = v.match_replace(exr[:, tb, 0:NE + 2], want[:, tb, :], chx[:, tb, 0:NE + 2], TAKEN)
                link(ins)
                v.tensor_scalar(taken, exr[:, :, 0:NE], TAKEN, None, ALU.is_equal).then_inc(S("taken"), 1)
                v.memset(gates[:], 0.0)
                v.memset(posm[:], FAR)
                dve.wait_ge(S("taken"), L + 1)
                link(v.tensor_tensor(cho, sco, taken, ALU.mult))
                link(v.tensor_reduce(norm[:, 0:2], cho, AX.X, ALU.add))
                link(v.reciprocal(norm[:, 2:4], norm[:, 0:2]))
                for tb in range(TB):
                    v.tensor_scalar(gates[:, tb, 0:NE], cho[:, tb, :], norm[:, 2 + tb:3 + tb], SCALE, ALU.mult, ALU.mult)
                link(v.tensor_scalar(exr[:, :, 0:NE], taken, -FAR, FAR, ALU.mult, ALU.add))
                for m in range(2):
                    ps = bank_read(dve, ("sgu", L, m))
                    dve.wait_ge(S("silS"), 2 * L + m + 1)
                    bank_done(v.tensor_tensor(hidS[:, m, :], silS[:, m, :], ps[:, T:2 * T], ALU.mult), ("sgu", L, m))
                ps = bank_read(dve, ("pos", L))
                v.tensor_tensor(posm[:, :, 0:NE], exr[:, :, 0:NE], ps[:, 0:TB * NE].rearrange("p (a e) -> p a e", a=TB), ALU.add)
                ins = v.tensor_reduce(norm[:, 0:1], ps[:, TB * NE:3 * NE], AX.X, ALU.max)
                bank_done(ins, ("pos", L))
                bank_moved(dve, ("pos", L))
                link(v.tensor_scalar(norm[:, 1:2], norm[:, 0:1], float(SLOTS), None, ALU.is_gt))
                link(v.scalar_tensor_tensor(norm[:, 2:3], norm[:, 0:1], 2.0 * SLOTS, norm[:, 1:2], ALU.is_gt, ALU.add))
                v.scalar_tensor_tensor(rounds[:], norm[:, 0:1], 3.0 * SLOTS, norm[:, 2:3], ALU.is_gt, ALU.add)\
                 .then_inc(S("rounds"), 1)

                def select(lp, g, off):
                    cell = [P, TB, GE, SLOTS]
                    where = posm[:, :, bass.ds(g, GE)] if not isinstance(g, int) else posm[:, :, g:g + GE]
                    gate = gates[:, :, bass.ds(g, GE)] if not isinstance(g, int) else gates[:, :, g:g + GE]
                    grid = iota[:].unsqueeze(1).unsqueeze(1).to_broadcast(cell)
                    v.tensor_tensor(pick.rearrange("p a (j s) -> p a j s", j=GE),
                                    where.unsqueeze(3).to_broadcast(cell), grid, ALU.is_equal).then_inc(lp.sem("pick"), 1)
                    dve.wait_ge(lp.sem("pick"), off)
                    v.tensor_tensor(pickg.rearrange("p a (j s) -> p a j s", j=GE),
                                    pick.rearrange("p a (j s) -> p a j s", j=GE),
                                    gate.unsqueeze(3).to_broadcast(cell), ALU.mult).then_inc(lp.sem("pick"), 1)

                for tb in range(TB):
                    row = xrow[:, tb, :]
                    link(v.tensor_copy(xs[0][:, tb, :], row))
                    link(v.tensor_tensor(rest, row, xs[0][:, tb, :], ALU.subtract))
                    link(v.tensor_copy(xs[1][:, tb, :], rest))
                    ins = v.tensor_tensor(xs[2][:, tb, :], rest, xs[1][:, tb, :], ALU.subtract)
                    if tb == 0:
                        link(ins)
                    else:
                        ins.then_inc(S("xs"), 1)
                dve.wait_ge(S("consts"), 6)

                def gathered(read, done, key):
                    c = key[-1]
                    ps = read(dve, key)
                    done(v.tensor_copy(xg[:, c, :], ps[:, 0:GSLOT]), key)

                def group(lp):
                    lp.read(dve, "gT")
                    select(lp, lp.i * GE + GE, lp.count(2, 2, 1))

                    def hidden(pr):
                        ps = lp.read(dve, ("gu", pr))
                        dve.wait_ge(lp.sem("silu"), lp.count(GE // 2, 0, pr + 1))
                        lp.done(v.tensor_tensor(hid[pr], hid[pr], ps[:, HID:2 * HID], ALU.mult), ("gu", pr))

                    def rows(pr):
                        ps = lp.read(dve, ("dn", pr, 1))
                        lp.done(v.tensor_copy(y[:, pr, HALF:], ps[:]), ("dn", pr, 1))

                    hidden(0)
                    hidden(1)
                    gathered(lp.read, lp.done, ("gather", 1))
                    rows(0)
                    gathered(lp.read, lp.done, ("gather", 3))
                    gathered(lp.read, lp.done, ("gather", 5))
                    rows(1)
                    gathered(lp.read, lp.done, ("gather", 7))
                    for n in range(4):
                        tb, h = divmod(n, 2)
                        ps = lp.read(dve, ("scatter", n))
                        part = acc[:, tb, HALF * h:HALF * h + HALF]
                        lp.done(v.tensor_tensor(part, part, ps[:], ALU.add), ("scatter", n))

                lp = ExpertLoop(L, banks, S, bank)
                link(v.memset(st[:], 0.0))
                select(lp, 0, 1)
                for c in range(1, C, 2):
                    gathered(bank_read, bank_done, ("gather", L, c))
                for tb in range(TB):
                    for h in range(2):
                        bank_moved(dve, ("sdn", L, tb, h))
                with dve.Fori(0, NGRP) as i:
                    lp.i = i
                    group(lp)
                dve.wait_ge(S("rounds"), L + 1)
                more = dve.value_load(rounds[0:1, 0:1], min_val=0, max_val=MAXR - 1)
                with dve.If(more > 0):
                    with dve.Fori(0, more) as r:
                        lp = ExpertLoop(L, banks, S, bank, r)
                        v.tensor_scalar(posm[:], posm[:], -float(SLOTS), None, ALU.add).then_inc(lp.sem("round"), 1)
                        dve.wait_ge(lp.sem("round"), r + 1)
                        select(lp, 0, lp.count(2, 2, -1))
                        for c in range(1, C, 2):
                            gathered(lp.read, lp.done, ("first", c))
                        with dve.Fori(0, NGRP) as i:
                            lp.i = i
                            group(lp)
                    n = NGRP * banks.per[L][GATHER_BANKS[0]] + C // 2
                    dve.wait_ge(S(f"more{L}_free{GATHER_BANKS[0]}"), more * n + 1)
                    v.memset(st[:], 0.0).then_inc(S(f"more{L}_round"), 1)
                with dve.Else():
                    dve.nop()
                for b in range(8):
                    dve.wait_ge(S(f"bank_free{b}"), banks.base[L][b] + NGRP * banks.per[L][b])
                for tb in range(TB):
                    link(v.scalar_tensor_tensor(xrow[:, tb, :], xrow[:, tb, :], ALPHA, acc[:, tb, :], ALU.mult, ALU.add))
                    if tb == 0:
                        dve.wait_ge(S(f"ln2par{L}"), 32)
                    layer_norm(tb, 2 * L + 1, 3, 4)

        def prog_gpsimd(pool):
            g = nc.gpsimd

            g.memset(ident[:], 0.0).then_inc(S("ident"), 1)
            pool.wait_ge(S("ident"), 1)
            g.affine_select(out=ident[:], in_=ident[:], compare_op=ALU.not_equal, fill=1.0, base=0,
                            pattern=[[-1, P]], channel_multiplier=1).then_inc(S("ident"), 1)
            g.memset(half[:], -0.5).then_inc(S("half"), 1)
            for k in range(ROPE // 2):
                ins = g.memset(freq[:, k:k + 1], float(FREQ[k]))
            ins.then_inc(S("freq"), 1)
            g.memset(mask[:], 0.0).then_inc(S("consts"), 1)
            g.memset(before[:], 1.0).then_inc(S("consts"), 1)
            g.memset(ones[:], 1.0).then_inc(S("consts"), 1)
            g.iota(iota[:], pattern=[[1, SLOTS]], base=0, channel_multiplier=0,
                   allow_small_or_imprecise_dtypes=True).then_inc(S("consts"), 1)
            pool.wait_ge(S("consts"), 4)
            g.affine_select(out=mask[:, P:T], in_=mask[:, P:T], compare_op=ALU.is_ge, fill=NEG, base=0,
                            pattern=[[-1, P]], channel_multiplier=1).then_inc(S("consts"), 1)
            g.affine_select(out=before[:], in_=before[:], compare_op=ALU.is_gt, fill=0.0, base=0,
                            pattern=[[1, P]], channel_multiplier=-1).then_inc(S("consts"), 1)

            done_roots = [0]

            def power(ap):
                done_roots[0] += 1
                pool.wait_ge(S("variance"), done_roots[0])
                g.tensor_tensor(ap, ap, half[:, 0:ap.shape[-1]], ALU.pow).then_inc(S("inv_std"), 1)

            def params(L, k, name):
                g.dma_start(par[:, k, :], bcast(I[f"l{L}_{name}"]))\
                 .then_inc(S(f"{'par' if k < 3 else 'ln2par'}{L}"), 16)

            def router(L):
                g.dma_start(rw[:], I[f"l{L}_router_w"].rearrange("(p c) n -> p c n", c=C)).then_inc(S("router_w"), 16)
                g.dma_start(rbias[:], bcast(I[f"l{L}_router_bias"])).then_inc(S("router_w"), 16)

            for k, name in enumerate(("b_out", "ln1_g", "ln1_b")):
                params(0, k, name)
            router(0)
            with nc.allow_non_contiguous_dma(reason="16 forget columns"):
                g.dma_start(wf[:], I["l1_w_in"].rearrange("(p c) n -> p c n", c=C)[:, :, 3 * D:]).then_inc(S("wf"), 16)
            pool.wait_ge(S("half"), 1)
            for tb in range(TB):
                power(norm[:, 2 * tb:2 * tb + 2])
            j = CC - 1
            bank_moved(pool, ("ag", j))
            w = 12 + TAPS * j
            g.tensor_scalar(uacc[:, j, :], upad[:, j, 0:T], cols[:, w:w + 1], cols[:, 8 + j:9 + j],
                            ALU.mult, ALU.add).then_inc(S("conv_pool"), 1)
            for k in range(1, TAPS):
                g.tensor_scalar(tapped[:, k % 2, :], upad[:, j, k:k + T], cols[:, w + k:w + k + 1], None,
                                ALU.mult).then_inc(S("tapped"), 1)
                pool.wait_ge(S("tapped"), k)
                pool.wait_ge(S("conv_pool"), k)
                g.tensor_tensor(uacc[:, j, :], uacc[:, j, :], tapped[:, k % 2, :], ALU.add)\
                 .then_inc(S("conv_pool"), 1)
            def scale_x(L):
                for k in range(4):
                    bank_read(pool, ("xt", 2 * L, k))
                pool.wait_ge(S(f"par{L}"), 48)
                for tb in range(TB):
                    g.tensor_scalar(xrow[:, tb, :], xrow[:, tb, :], ALPHA, None, ALU.mult).then_inc(S("scaled"), 1)
                    pool.wait_ge(S("scaled"), 4 * L + 2 * tb + 1)
                    g.tensor_tensor(xrow[:, tb, :], xrow[:, tb, :], par[:, 0, :], ALU.add).then_inc(S("scaled"), 1)

            pool.wait_ge(S("conv_pool"), TAPS)
            for k, name in ((3, "ln2_g"), (4, "ln2_b")):
                params(0, k, name)
            scale_x(0)
            for _ in range(2):
                for tb in range(TB):
                    power(rstd[:, tb:tb + 1])
            pool.wait_ge(S("ln_done"), 2)
            for k, name in enumerate(("b_out", "ln1_g", "ln1_b")):
                params(1, k, name)
            bank_read(pool, ("router", 0))
            pool.wait_ge(S("taken"), 1)
            router(1)
            for tb in range(TB):
                power(rstd[:, tb:tb + 1])
            pool.wait_ge(S("ln_done"), 4)
            for a in (qT, kT):
                g.memset(a[HD:HD + 2, :, :], 1.0).then_inc(S("unit_rows"), 1)
            g.dma_start(vbias, bcast(I["l1_b_in"][2 * D:3 * D])).then_inc(S("vbias"), 16)
            for k, name in ((3, "ln2_g"), (4, "ln2_b")):
                params(1, k, name)
            pool.wait_ge(S("unit_rows"), 2)
            pool.wait_ge(S("decay"), 1)
            g.dma_start(qT[HD:HD + 1, :, :], fg[3][0:H1]).then_inc(S("decay_rows"), 16)
            g.dma_start(kT[HD + 1:HD + 2, :, :], fg[4][0:H1]).then_inc(S("decay_rows"), 16)
            scale_x(1)
            for _ in range(2):
                for tb in range(TB):
                    power(rstd[:, tb:tb + 1])

        with nc.Block() as block:
            @block.sync
            def _(sp):
                prog_sync(sp)

            @block.tensor
            def _(pe):
                prog_tensor(pe)

            @block.scalar
            def _(act):
                prog_scalar(act)

            @block.vector
            def _(dve):
                prog_vector(dve)

            @block.gpsimd
            def _(pool):
                prog_gpsimd(pool)


def kernel(**inputs):
    import concourse.bacc as bacc
    from concourse.bass_utils import run_bass_kernel_spmd

    nc = bacc.Bacc("TRN2", target_bir_lowering=False, num_devices=1)
    arrays, I = {}, {}
    for name, a in inputs.items():
        a = np.ascontiguousarray(a)
        arrays[f"in_{name}"] = a
        I[name] = nc.dram_tensor(f"in_{name}", a.shape, mybir.dt.from_np(a.dtype), kind="ExternalInput").ap()
    out = nc.dram_tensor("out_0", (1, T, D), F32, kind="ExternalOutput").ap()
    program(nc, I, out)
    return run_bass_kernel_spmd(nc, [arrays], core_ids=[0]).results[0]["out_0"]
```

```python
from contextlib import ExitStack

import numpy as np

import concourse.bass as bass
from concourse import mybir

F32 = mybir.dt.float32
BF16 = mybir.dt.bfloat16
I32 = mybir.dt.int32
ALU = mybir.AluOpType
ACT = mybir.ActivationFunctionType
AX = mybir.AxisListType

P = 128
D = 1024
T = 256
TB = T // P
C = D // P
HALF = 512
ALPHA = 4.0 ** 0.25
LN_EPS, RMS_EPS = 1e-5, 1e-6

CONV, TAPS = 512, 31
CC = CONV // P
POOL_CHUNK, PE_CHUNK = 2, 3
DVE_CHUNKS = 2
POOL_FROM, PE_FROM = 2, 3
EARLY = 20
DVE_CUTS = (0, 5, 10, 14, 18, 21, 24, 27, 29, TAPS)
H0, NOPE, ROPE, VD = 8, 64, 32, 64
QK = NOPE + ROPE
QL, KVL = 256, 128
LAT = QL + KVL + ROPE
H1, HD = 16, 64

NE, TOPK, NG, TOPG, HID = 64, 6, 8, 4, 256
GS = NE // NG
SCALE = 2.5
SLOTS = 64
GE = 4
NGRP = NE // GE
GSLOT = GE * SLOTS
MAXR = T // SLOTS
UNROLL = 2

NEG = -1e30
SENT = -2e30
TAKEN = 3e38
FAR = 1e6

NU = 12
UNIT = 2048
GATHER_BANKS = (4, 5)

ROUND = 1.5 * 2.0 ** 23
TWO_PI = (6.28125, 0.0019350051879882812, 3.0199159819567e-07)
FREQ = (1.0 / (np.float32(10000.0) ** (np.arange(0, ROPE, 2, dtype=np.float32) / np.float32(ROPE)))).astype(np.float32)


class Plan:

    def __init__(self):
        self.n, self.at, self.per, self.base, self.end = {}, {}, {}, {}, {}

    def add(self, key, res):
        self.at[key] = (res, self.n.get(res, 0))
        self.n[res] = self.n.get(res, 0) + 1

    def loop(self, name, seq, times, but=()):
        self.base[name], per = dict(self.n), {}
        for key, res in seq:
            self.at[(name, key)] = (res, self.n.get(res, 0), per.get(res, 0))
            per[res] = per.get(res, 0) + 1
        self.per[name] = per
        for res, k in per.items():
            self.n[res] = self.n.get(res, 0) + k * times
        for key, res in seq:
            self.n[res] -= key[0] in but
        self.end[name] = dict(self.n)


def plan_banks():
    u = Plan()

    def xt(n):
        for k in range(4):
            u.add(("xt", n, k), k)

    def attention(L, heads):
        for h in range(heads):
            u.add(("score", L, h), h % 2)
            u.add(("pt", L, h), 2 + h % 2)
            if h % 2:
                u.add(("ot", L, h // 2), 4)

    u.add("cols0", 7)
    xt(0)
    for tb in range(TB):
        u.add(("lat", tb), 4 + tb)
    u.add(("ag", 0), 6)
    for tb in range(TB):
        u.add(("latT", tb), 2 + tb)
    for tb in range(TB):
        for h in range(2):
            u.add(("q", tb, h), [4, 5, 7, 6][2 * tb + h])
    for tb in range(TB):
        for h in range(2):
            u.add(("kv", tb, h), 2 * tb + h)
    u.add(("ag", 1), 4)
    for tb in range(TB):
        for g in range(2):
            u.add(("kT", tb, g), 2 * tb + g)
    for tb in range(TB):
        for g in range(2):
            u.add(("qT", tb, g), [6, 7, 4, 5][2 * tb + g])
    u.add(("ag", 2), 6)
    u.add(("ag", 3), 7)
    u.add("convT", 5)
    attention(0, H0)
    for tb in range(TB):
        u.add(("urow", tb), 6 + tb)
    for tb in range(TB):
        for h in range(2):
            u.add(("mix", 0, tb, h), 2 * tb + h)
    for tb in range(TB):
        u.add(("uT", tb), 4 + tb)
    for L in range(2):
        if L == 1:
            xt(2)
            u.add("cols1", 4)
            u.add("forget", 0)
            for b in range(H1 // 4):
                u.add(("qk", b), 5)
                u.add(("qk", 4 + b), 6)
                u.add(("v", b), 7)
            attention(1, H1)
            for tb in range(TB):
                for h in range(2):
                    u.add(("mix", L, tb, h), [5, 6, 7, 0][2 * tb + h])
        xt(1 + 2 * L)
        u.add(("router", L), 4)
        for m in range(2):
            u.add(("sgu", L, m), m)
        u.add(("pos", L), 5)
        for tb in range(TB):
            for h in range(2):
                u.add(("sdn", L, tb, h), [2, 3, 6, 7][2 * tb + h])
        for c in range(C):
            u.add(("gather", L, c), GATHER_BANKS[c % 2])
        seq = [("gT", 2)]
        seq += [(("gu", pr), pr) for pr in range(GE // 2)]
        seq += [(("hT", pr), pr) for pr in range(GE // 2)]
        seq += [(("dn", pr, h), 2 + h) for pr in range(GE // 2) for h in range(2)]
        seq += [(("gather", c), GATHER_BANKS[c % 2]) for c in range(C)]
        seq += [(("scatter", n), [7, 6][n % 2]) for n in range(4)]
        u.loop(L, seq, NGRP, but=("gather",))
    return u


def plan_units():
    u = Plan()
    for k in range(4):
        u.add(("in0", k), k)
    u.add(("lat", 0), 4)
    u.add("uq", 6)
    u.add("ukv", 7)
    for k in range(4):
        u.add(("out0", k), 8 + k)
    for k in range(3):
        u.add(("shared", 0, k), k)
    first = {0: 1, 1: 0}
    u.loop(0, [((j, k), 3 * ((first[0] + j) % 4) + k) for j in range(GE) for k in range(3)], NGRP)
    for k in range(12):
        u.add(("in1", k), (3 + k) % 12)
    for k in range(4):
        u.add(("out1", k), 3 + k)
    for k in range(3):
        u.add(("shared", 1, k), 9 + k)
    u.loop(1, [((j, k), 3 * ((first[1] + j) % 4) + k) for j in range(GE) for k in range(3)], NGRP)
    return u


class ExpertLoop:

    def __init__(self, L, banks, S, bank, r=None, step=1):
        self.L, self.plan, self.S, self.tiles, self.r, self.step = L, banks, S, bank, r, step
        self.i, self.u = None, 0
        self.tag = f"{'moe' if r is None else 'more'}{L}"

    def groups(self, per, more):
        return self.i * (per * self.step) + (self.u * per + more)

    def sem(self, name):
        return self.S(f"{self.tag}_{name}")

    def count(self, per, prologue, off):
        n = prologue + off if self.i is None else self.groups(per, prologue + off)
        return n if self.r is None else self.r * (NGRP * per + prologue) + n

    def at(self, key, back=0):
        b, base, off = self.plan.at[(self.L, key)]
        per = self.plan.per[self.L][b]
        if self.r is None:
            return b, self.S(f"bank_full{b}"), self.S(f"bank_free{b}"), self.groups(per, base + off - back * per)
        pro = C // 2 if b in GATHER_BANKS else 0
        return b, self.sem(f"full{b}"), self.sem(f"free{b}"), self.count(per, pro, off - back * per)

    def at_prologue(self, c):
        b = GATHER_BANKS[c % 2]
        per = self.plan.per[self.L][b]
        return b, self.sem(f"full{b}"), self.sem(f"free{b}"), self.r * (NGRP * per + C // 2) + c // 2

    def where(self, key):
        return self.at_prologue(key[1]) if key[0] == "first" else self.at(key)

    def open(self, pe, key):
        b, _, free, n = self.where(key)
        pe.wait_ge(free, n if self.r is None else n + 1)
        return self.tiles[b]

    def made(self, ins, key):
        ins.then_inc(self.where(key)[1], 1)

    def read(self, eng, key):
        b, full, _, n = self.where(key)
        eng.wait_ge(full, n + 1)
        return self.tiles[b]

    def done(self, ins, key):
        ins.then_inc(self.where(key)[2], 1)

    def moved(self, eng, key):
        _, _, free, n = self.where(key)
        eng.wait_ge(free, n + 1 if self.r is None else n + 2)


def run_groups(eng, lp, group, whole=False):
    bodies = NGRP // UNROLL
    lp.step = UNROLL
    with eng.Fori(0, bodies if whole else bodies - 1) as i:
        for u in range(UNROLL):
            lp.i, lp.u = i, u
            group(lp)
    if not whole:
        for u in range(UNROLL):
            lp.i, lp.u = bodies - 1, u
            group(lp, last=u == UNROLL - 1)


def last_use_of_weights(j, w):
    return ("gu", j // 2) if w < 2 else ("dn", j // 2, 1)


def weights_of(j, w):
    return f"{'gu' if w < 2 else 'dn'}_weights{j // 2}"


IN_ORDER = [(j, w) for j in range(GE) for w in range(2)] + [(j, 2) for j in range(GE)]


def program(nc, I, out):
    banks, units = plan_banks(), plan_units()
    with ExitStack() as ctx:
        def sb(name, shape, dt=F32):
            return ctx.enter_context(nc.sbuf_tensor(name, shape, dt))

        sems = {}

        def S(name):
            if name not in sems:
                sems[name] = ctx.enter_context(nc.semaphore(name))
            return sems[name]

        bank = [ctx.enter_context(nc.psum_tensor(f"bank{b}", [P, HALF], F32)) for b in range(8)]
        ring = sb("ring", [P, NU * UNIT])
        xrow = sb("xrow", [P, TB, D])
        xT = sb("xT", [P, C, T])
        mixT = sb("mixT", [P, C, T])
        big = sb("big", [P, 8192])
        V = sb("V", [P, TB * D])
        par = sb("par", [P, 5, D])
        side = sb("side", [P, 3072])
        att = sb("att", [P, 1536])
        rw = sb("rw", [P, C, NE])
        wf = sb("wf", [P, C, H1])
        ident = sb("ident", [P, P])
        mask = sb("mask", [P, T])
        iota = sb("iota", [P, SLOTS])
        before = sb("before", [P, P], BF16)
        ones = sb("ones", [P, P], BF16)
        rbias = sb("rbias", [P, NE])
        cols = sb("cols", [P, 12 + CC * TAPS])
        qkcol = sb("qkcol", [P, 2, 16])
        rows1 = sb("rows1", [16, P])
        fbias = sb("fbias", [H1, 1])
        posi = sb("posi", [P, TB], I32)
        posf = sb("posf", [P, TB])
        freq = sb("freq", [P, ROPE // 2])
        turn = sb("turn", [P, 2, TB, ROPE // 2])
        st = sb("st", [P, 2, 12])
        mv = sb("mv", [P, 4])
        rstd = sb("rstd", [P, 4])
        mx = sb("mx", [P, 2, 4])
        rs = sb("rs", [P, 2, 4])
        posm = sb("posm", [P, TB, NE + GE])
        gates = sb("gates", [P, TB, NE + GE])
        gsx = sb("gsx", [P, TB, 12])
        gsr = sb("gsr", [P, TB, 12])
        top = sb("top", [P, TB, 8])
        want = sb("want", [P, TB, 8])
        pen = sb("pen", [P, TB, NG])
        half = sb("half", [P, 2])
        spare = sb("spare", [P, 1])
        norm = sb("norm", [P, 4])
        gcol = sb("gcol", [P, 2])
        rounds = sb("rounds", [P, 1], I32)

        def cut(area, at, *shape):
            n = int(np.prod(shape))
            v = area[:, at:at + n]
            if len(shape) == 2:
                return v.rearrange("p (a b) -> p a b", a=shape[0])
            if len(shape) == 3:
                return v.rearrange("p (a b c) -> p a b c", a=shape[0], b=shape[1])
            return v

        qT, kT = cut(big, 0, H1, T), cut(big, 4096, H1, T)
        qT0, kT0 = cut(big, 0, H0, T), cut(big, 2048, H0, T)
        qrow, krow = cut(big, 4096, TB, H0, QK), cut(big, 5632, TB, H0, QK)
        lat = cut(big, 7168, TB, LAT)
        V0, V1 = cut(V, 0, TB, H0 * VD), cut(V, 0, TB, D)
        cln = cut(V, 1024, 2, CONV)
        upad, urow = cut(side, 0, CC, TAPS - 1 + T), cut(side, 0, TB, CONV)
        uacc = cut(side, 1144, CC, T)
        lpar = cut(side, 2168, LAT + QL + KVL)
        vbias = cut(side, 0, D)
        latT = mixT[:, 0:3, :]
        rows0, taps0 = mixT[0:12, 3, 0:P], mixT[0:TAPS, 4:6, :].rearrange("p a b -> p (a b)")
        tapped = par[:, 3, 0:4 * T].rearrange("p (a t) -> p a t", a=4)
        ang = cut(att, 0, 2, TB, ROPE // 2)
        rt = [cut(att, 256 * k, TB, H0, ROPE // 2) for k in range(4)]
        fg = [cut(att, 256 * k, T) for k in range(5)]
        sc = [cut(att, 0, 384), cut(att, 384, 384), cut(side, 2560, 384)]
        pt = [cut(att, 768 + 384 * b, 384) for b in range(2)]
        diag = ring[:, 4 * UNIT:4 * UNIT + TAPS * P].rearrange("p (k n) -> p k n", k=TAPS)
        acc = mixT[:, :, :].rearrange("p c t -> p (c t)").rearrange("p (a b) -> p a b", a=TB)
        xs = [side[:, 1024 * k:1024 * k + 1024].bitcast(BF16).rearrange("p (a b) -> p a b", a=TB) for k in range(3)]
        xg = cut(big, 0, C, GSLOT)
        ys = [big[:, at:at + 1024].bitcast(BF16).rearrange("p (a b) -> p a b", a=2) for at in (2048, 3072, 6656)]
        hot = big[:, 7680:7680 + T].bitcast(BF16).rearrange("p (a t) -> p a t", a=2)
        gT = cut(big, 4096, 2, T)
        hidT = [cut(big, 4608 + 256 * pr, 2, P) for pr in range(GE // 2)]
        hid = [cut(big, 5120 + 256 * pr, HID) for pr in range(GE // 2)]
        hidS, silS = cut(big, 5632, 2, T), cut(big, 6144, 2, T)
        rest = [cut(V, D * n, D) for n in range(2)]
        pick = att[:, 0:GSLOT].bitcast(BF16).rearrange("p (a b) -> p a b", a=TB)
        pickg = cut(att, 256, TB, GSLOT)
        sco, cho = cut(att, 768, TB, NE), cut(att, 896, TB, NE)
        chx, exr = cut(att, 1024, TB, 72), cut(att, 1168, TB, 72)
        m8 = cut(att, 1312, TB, NG, 8)
        taken = att[:, 1440:1504].bitcast(BF16).rearrange("p (a b) -> p a b", a=TB)

        def unit(key):
            u = units.at[key][0]
            return ring[:, u * UNIT:(u + 1) * UNIT]

        def by_chunk(u):
            return u.rearrange("p (c f) -> p c f", c=C)

        def by_pair(u):
            return u.rearrange("p (m n) -> p m n", m=2)

        def bank_open(pe, key):
            b, n = banks.at[key]
            if n:
                pe.wait_ge(S(f"bank_free{b}"), n)
            return bank[b]

        def bank_made(ins, key):
            ins.then_inc(S(f"bank_full{banks.at[key][0]}"), 1)

        def bank_read(eng, key):
            b, n = banks.at[key]
            eng.wait_ge(S(f"bank_full{b}"), n + 1)
            return bank[b]

        def bank_done(ins, key):
            ins.then_inc(S(f"bank_free{banks.at[key][0]}"), 1)

        def bank_moved(eng, key):
            b, n = banks.at[key]
            eng.wait_ge(S(f"bank_free{b}"), n + 1)

        def unit_wait(pe, key):
            u, n = units.at[key]
            pe.wait_ge(S(f"unit_full{u}"), 16 * (n + 1))

        def bcast(ap, n=P):
            return ap.partition_broadcast(n)

        def loop_unit(L, j, w):
            return units.at[(L, (j, w))]

        def loop_weights(L, j, w):
            u = loop_unit(L, j, w)[0]
            a = ring[:, u * UNIT:(u + 1) * UNIT]
            return by_chunk(a) if w < 2 else by_pair(a)

        def prog_sync(sp):
            def load(key, dst, src, after=None):
                if after:
                    bank_read(sp, after)
                sp.dma_start(dst, src).then_inc(S(f"unit_full{units.at[key][0]}"), 16)

            def expert_weights(L, e, w):
                src = I[f"l{L}_exp_w_{('gate', 'up', 'down')[w]}"][bass.ds(e, 1)]
                return src.rearrange("a (p c) f -> (a p) c f", c=C) if w < 2 else \
                    src.rearrange("a (p m) n -> (a p) m n", m=2)

            for tb in range(TB):
                sp.dma_start(xrow[:, tb, :], I["x"][0, P * tb:P * tb + P, :]).then_inc(S(f"x_in{tb}"), 16)
            win = I["l0_w_in"].rearrange("(p c) n -> p c n", c=C)
            wl = ring[:, 4 * UNIT:4 * UNIT + C * LAT].rearrange("p (c n) -> p c n", c=C)
            load(("lat", 0), wl, win[:, :, 2 * CONV:])
            for k in (0, 2):
                load(("in0", k), by_chunk(unit(("in0", k))), win[:, :, 256 * k:256 * k + 256])
            load("uq", unit("uq")[:, 0:1536].rearrange("p (k n) -> p k n", k=2),
                 I["l0_w_uq"].rearrange("(k p) n -> p k n", p=P))
            load("ukv", unit("ukv")[:, 0:1024], I["l0_w_ukv"])
            for k in (1, 3):
                load(("in0", k), by_chunk(unit(("in0", k))), win[:, :, 256 * k:256 * k + 256])
            for L in range(2):
                if L == 1:
                    win = I["l1_w_in"].rearrange("(p c) n -> p c n", c=C)
                    for k in (0, 4, 1, 8, 5, 9, 2, 6, 10, 3, 7, 11):
                        j, w = divmod(k, 3)
                        b, base, off = banks.at[(0, last_use_of_weights(j, w))]
                        sp.wait_ge(S(f"bank_full{b}"), base + off + 1 + (NGRP - 1) * banks.per[0][b])
                        load(("in1", k), by_chunk(unit(("in1", k))), win[:, :, 256 * k:256 * k + 256])
                wout = I[f"l{L}_w_out"].rearrange("(k j p) n -> k p j n", p=P, j=2)
                for k in range(4):
                    load((f"out{L}", k), by_pair(unit((f"out{L}", k))), wout[k],
                         after=("qk", k) if L else None)
                for w, name in enumerate(("gate", "up", "down")):
                    src = I[f"l{L}_sh_w_{name}"]
                    a = unit(("shared", L, w))
                    before_it = ("ag", 3) if L == 0 else [("qk", 6), ("qk", 7), ("v", 0)][w]
                    if w < 2:
                        load(("shared", L, w), by_chunk(a), src.rearrange("(p c) f -> p c f", c=C), before_it)
                    else:
                        load(("shared", L, w), by_pair(a), src.rearrange("(m p) n -> p m n", p=P), before_it)
                mix, sgu, sdn = ("mix", L, 1, 1), ("sgu", L, 1), ("sdn", L, 1, 1)
                if L == 0:
                    held = [("ag", 3), "convT", "convT", ("q", 1, 1), ("kv", 1, 1), mix,
                            mix, mix, mix, sgu, sgu, sdn]
                else:
                    held = [("v", 1), ("v", 2), ("v", 3)] + [mix] * 4 + [("qk", 4), ("qk", 5), sgu, sgu, sdn]
                for j in range(GE):
                    for w in range(3):
                        bank_read(sp, held[3 * j + w])
                        sp.dma_start(loop_weights(L, j, w), expert_weights(L, j, w))\
                          .then_inc(S(f"unit_full{loop_unit(L, j, w)[0]}"), 16)
                lp = ExpertLoop(L, banks, S, bank)
                with sp.Fori(1, NGRP) as i:
                    lp.i = i
                    for j, w in IN_ORDER:
                        _, full, _, n = lp.at(last_use_of_weights(j, w), back=1)
                        sp.wait_ge(full, n + 1)
                        sp.dma_start(loop_weights(L, j, w), expert_weights(L, i * GE + j, w))\
                          .then_inc(S(f"unit_full{loop_unit(L, j, w)[0]}"), 16)
                sp.wait_ge(S("rounds"), L + 1)
                more = sp.value_load(rounds[0:1, 0:1], min_val=0, max_val=MAXR - 1)
                with sp.If(more > 0):
                    with sp.Fori(0, more) as r:
                        lp = ExpertLoop(L, banks, S, bank, r)
                        sp.wait_ge(lp.sem("round"), r + 1)
                        for j in range(GE):
                            for w in range(3):
                                sp.dma_start(loop_weights(L, j, w), expert_weights(L, j, w))\
                                  .then_inc(lp.sem(weights_of(j, w)), 16)
                        with sp.Fori(1, NGRP) as i:
                            lp.i = i
                            for j, w in IN_ORDER:
                                _, full, _, n = lp.at(last_use_of_weights(j, w), back=1)
                                sp.wait_ge(full, n + 1)
                                sp.dma_start(loop_weights(L, j, w), expert_weights(L, i * GE + j, w))\
                                  .then_inc(lp.sem(weights_of(j, w)), 16)
                    sp.wait_ge(S(f"more{L}_round"), more + 1)
                    sp.sem_inc(S("rounds_seen"), 1)
                with sp.Else():
                    sp.nop()
            for tb in range(TB):
                sp.wait_ge(S("ln_done"), 6 + tb + 1)
                sp.dma_start(out[0, P * tb:P * tb + P, :], xrow[:, tb, :]).then_inc(S("stored"), 16)
            sp.wait_ge(S("stored"), 32)

        def prog_tensor(pe):
            mm, flip = nc.tensor.matmul, nc.tensor.transpose

            def xt(n, tb):
                if n == 0:
                    pe.wait_ge(S(f"x_in{tb}"), 16)
                else:
                    pe.wait_ge(S("ln_done"), 2 * (n - 1) + tb + 1)
                rows = xrow[:, tb, :].rearrange("t (p c) -> t c p", c=C)
                for g in range(2):
                    key = ("xt", n, 2 * tb + g)
                    ps = bank_open(pe, key)
                    for k in range(4):
                        ins = flip(ps[:, P * k:P * k + P], rows[:, 4 * g + k, :], ident[:])
                    bank_made(ins, key)

            def xt_there(n, tb):
                for g in range(2):
                    bank_moved(pe, ("xt", n, 2 * tb + g))

            def attention(L, heads, dk, qt, kt, v, vd, between):
                def scores(h):
                    key = ("score", L, h)
                    ps = bank_open(pe, key)
                    mm(ps[:, 0:P], qt[0:dk, h, 0:P], kt[0:dk, h, 0:P], start=True, stop=True)
                    ins = mm(ps[:, P:P + T], qt[0:dk, h, P:T], kt[0:dk, h, :], start=True, stop=True)
                    bank_made(ins, key)

                scores(0)
                for h in range(heads + 2):
                    if h + 1 < heads:
                        if L == 1 and (h + 1) % 4 == 0:
                            for n in ((h + 1) // 4, 4 + (h + 1) // 4):
                                bank_moved(pe, ("qk", n))
                        scores(h + 1)
                    if h < heads:
                        between(h)
                    if 1 <= h <= heads:
                        g = h - 1
                        key = ("pt", L, g)
                        ps = bank_open(pe, key)
                        pe.wait_ge(S("probs"), (H0 if L else 0) + g + 1)
                        for k in range(3):
                            ins = flip(ps[:, P * k:P * k + P], sc[g % 3][:, P * k:P * k + P], ident[:])
                        bank_made(ins, key)
                    if h >= 2:
                        g = h - 2
                        key = ("ot", L, g // 2)
                        ps = bank_open(pe, key) if g % 2 == 0 else bank[banks.at[key][0]]
                        bank_moved(pe, ("pt", L, g))
                        if L == 1 and g % 4 == 0:
                            bank_moved(pe, ("v", g // 4))
                        r = slice(64 * (g % 2), 64 * (g % 2) + 64)
                        mm(ps[r, 0:T], v[:, 0, vd * g:vd * g + vd], pt[g % 2][:, 0:T], start=True, stop=False)
                        ins = mm(ps[r, P:T], v[:, 1, vd * g:vd * g + vd], pt[g % 2][:, T:T + P], start=False, stop=True)
                        if g % 2:
                            bank_made(ins, key)

            pe.wait_ge(S("ident"), 2)
            for tb in range(TB):
                xt(0, tb)
            for tb in range(TB):
                xt_there(0, tb)
            wl = ring[:, 4 * UNIT:4 * UNIT + C * LAT].rearrange("p (c n) -> p c n", c=C)
            unit_wait(pe, ("lat", 0))
            for tb in range(TB):
                ps = bank_open(pe, ("lat", tb))
                for c in range(C):
                    ins = mm(ps[:, 0:LAT], xT[:, c, P * tb:P * tb + P], wl[:, c, :], start=(c == 0), stop=(c == C - 1))
                bank_made(ins, ("lat", tb))
            pe.wait_ge(S("rows0"), 48)
            ps = bank_open(pe, "cols0")
            flip(ps[:, 0:12], rows0, ident[0:12, 0:12])
            for j in range(CC):
                ins = flip(ps[:, 12 + TAPS * j:12 + TAPS * j + TAPS], taps0[:, P * j:P * j + P], ident[0:TAPS, 0:TAPS])
            bank_made(ins, "cols0")

            def value_gate(j):
                key = ("ag", j)
                ps = bank_open(pe, key)
                for s in range(2):
                    w = by_chunk(unit(("in0", 2 * s + j // 2)))
                    unit_wait(pe, ("in0", 2 * s + j // 2))
                    for c in range(C):
                        ins = mm(ps[:, T * s:T * s + T], w[:, c, P * (j % 2):P * (j % 2) + P], xT[:, c, :],
                                 start=(c == 0), stop=(c == C - 1))
                bank_made(ins, key)

            value_gate(0)
            for tb in range(TB):
                pe.wait_ge(S("lat_normed"), tb + 1)
                ps = bank_open(pe, ("latT", tb))
                for k in range(3):
                    ins = flip(ps[:, P * k:P * k + P], lat[:, tb, P * k:P * k + P], ident[:])
                bank_made(ins, ("latT", tb))
            unit_wait(pe, "uq")
            wq = unit("uq")[:, 0:1536].rearrange("p (k n) -> p k n", k=2)
            for tb in range(TB):
                bank_moved(pe, ("latT", tb))
                for h in range(2):
                    ps = bank_open(pe, ("q", tb, h))
                    for k in range(2):
                        ins = mm(ps[:, 0:384], latT[:, k, P * tb:P * tb + P], wq[:, k, 384 * h:384 * h + 384],
                                 start=(k == 0), stop=(k == 1))
                    bank_made(ins, ("q", tb, h))
            unit_wait(pe, "ukv")
            for tb in range(TB):
                for h in range(2):
                    ps = bank_open(pe, ("kv", tb, h))
                    ins = mm(ps[:], latT[:, 2, P * tb:P * tb + P], unit("ukv")[:, HALF * h:HALF * h + HALF],
                             start=True, stop=True)
                    bank_made(ins, ("kv", tb, h))
            value_gate(1)
            for name, rows in (("kT", krow), ("qT", qrow)):
                pe.wait_ge(S(f"{name}_rows"), 1)
                if name == "kT":
                    for tb in range(TB):
                        for h in range(2):
                            bank_moved(pe, ("kv", tb, h))
                for tb in range(TB):
                    for g in range(2):
                        ps = bank_open(pe, (name, tb, g))
                        for k in range(4):
                            ins = flip(ps[0:QK, P * k:P * k + P], rows[:, tb, 4 * g + k, :], ident[:])
                        bank_made(ins, (name, tb, g))
            for name in ("qT", "kT"):
                for tb in range(TB):
                    for g in range(2):
                        bank_moved(pe, (name, tb, g))

            def conv(h):
                if h < 2:
                    value_gate(2 + h)
                if h < PE_FROM:
                    return
                if h == PE_FROM:
                    bank_open(pe, "convT")
                    bank_moved(pe, ("ag", PE_CHUNK))
                    pe.wait_ge(S("diagonals"), 1)
                steps = H0 - PE_FROM
                for k in range(TAPS * (h - PE_FROM) // steps, TAPS * (h - PE_FROM + 1) // steps):
                    ins = mm(bank[banks.at["convT"][0]][:, 0:T], diag[:, k, :], upad[:, PE_CHUNK, k:k + T],
                             start=(k == 0), stop=(k == TAPS - 1))
                if h == H0 - 1:
                    bank_made(ins, "convT")

            attention(0, H0, QK, qT0, kT0, V0, VD, conv)
            bank_moved(pe, "convT")
            pe.wait_ge(S("conv_dve"), 1)
            pe.wait_ge(S("conv_pool"), TAPS)
            for tb in range(TB):
                ps = bank_open(pe, ("urow", tb))
                for k in range(CC):
                    ins = flip(ps[:, P * k:P * k + P], uacc[:, k, P * tb:P * tb + P], ident[:])
                bank_made(ins, ("urow", tb))

            def mix(L, tb, h, ks, first=True, last=True):
                key = ("mix", L, tb, h)
                ps = bank_open(pe, key) if first else bank[banks.at[key][0]]
                for k in ks:
                    unit_wait(pe, (f"out{L}", k))
                    w = by_pair(unit((f"out{L}", k)))
                    for j in range(2):
                        start, stop = first and (k, j) == (ks[0], 0), last and (k, j) == (ks[-1], 1)
                        ins = mm(ps[:], mixT[:, 2 * k + j, P * tb:P * tb + P],
                                 w[:, j, HALF * h:HALF * h + HALF], start=start, stop=stop)
                if last:
                    bank_made(ins, key)

            for g in range(H0 // 2):
                bank_moved(pe, ("ot", 0, g))
            for tb in range(TB):
                for h in range(2):
                    mix(0, tb, h, (2, 3), last=False)
            for tb in range(TB):
                pe.wait_ge(S("u_act"), tb + 1)
                ps = bank_open(pe, ("uT", tb))
                for k in range(CC):
                    ins = flip(ps[:, P * k:P * k + P], urow[:, tb, P * k:P * k + P], ident[:])
                bank_made(ins, ("uT", tb))

            for L in range(2):
                if L == 1:
                    xt(2, 0)
                    pe.wait_ge(S("rows1"), 16)
                    ps = bank_open(pe, "cols1")
                    ins = flip(ps[:, 0:16], rows1[:], ident[0:16, 0:16])
                    bank_made(ins, "cols1")

                    def project(n, s, tbs=range(TB)):
                        unit_wait(pe, ("in1", n))
                        w = by_chunk(unit(("in1", n)))
                        key = ("qk", n) if n < 8 else ("v", n - 8)
                        t = slice(P * tbs[0], P * tbs[-1] + P)
                        ps = bank_open(pe, key) if s == 0 and t.start == 0 else bank[banks.at[key][0]]
                        for c in range(C):
                            if n < 8:
                                ins = mm(ps[:, T * s + t.start:T * s + t.stop], w[:, c, P * s:P * s + P], xT[:, c, t],
                                         start=(c == 0), stop=(c == C - 1))
                            else:
                                ins = mm(ps[:, T * s:T * s + T], xT[:, c, P * s:P * s + P], w[:, c, :],
                                         start=(c == 0), stop=(c == C - 1))
                        if s and t.stop == T:
                            bank_made(ins, key)

                    def between(h):
                        b, step = divmod(h, 4)
                        if b + 1 < H1 // 4:
                            for n, s in (((b + 1, 0), (b + 1, 1)), ((b + 5, 0), (b + 5, 1)),
                                         ((b + 9, 0),), ((b + 9, 1),))[step]:
                                project(n, s)
                        elif step < 3:
                            if step == 0:
                                for g in range(4):
                                    bank_moved(pe, ("ot", 1, g))
                            mix(1, step // 2, step % 2, (0, 1), last=False)
                        else:
                            for g in (4, 5):
                                bank_moved(pe, ("ot", 1, g))
                            for n in range(3):
                                mix(1, n // 2, n % 2, (2,), first=False, last=False)

                    xt_there(2, 0)
                    for n in (0, 4):
                        for s in range(2):
                            project(n, s, (0,))
                    project(8, 0)
                    xt(2, 1)
                    xt_there(2, 1)
                    pe.wait_ge(S("wf"), 16)
                    ps = bank_open(pe, "forget")
                    for c in range(C):
                        ins = mm(ps[0:H1, 0:T], wf[:, c, :], xT[:, c, :], start=(c == 0), stop=(c == C - 1))
                    bank_made(ins, "forget")
                    for n in (0, 4):
                        for s in range(2):
                            project(n, s, (1,))
                    project(8, 1)
                    for n in (0, 4):
                        bank_moved(pe, ("qk", n))
                    pe.wait_ge(S("decay_rows"), 32)
                    attention(1, H1, HD + 2, qT, kT, V1, HD, between)
                    mix(1, 1, 1, (0,), last=False)
                    for g in (6, 7):
                        bank_moved(pe, ("ot", 1, g))
                if L == 0:
                    for tb in range(TB):
                        bank_moved(pe, ("uT", tb))
                for tb in range(TB):
                    for h in range(2):
                        ks = (0, 1) if L == 0 else (1, 2, 3) if tb and h else (3,)
                        mix(L, tb, h, ks, first=False)

                def shared_gate_up(tb):
                    for m in range(2):
                        ps = bank_open(pe, ("sgu", L, m)) if tb == 0 else bank[banks.at[("sgu", L, m)][0]]
                        for s in range(2):
                            unit_wait(pe, ("shared", L, s))
                            w = by_chunk(unit(("shared", L, s)))
                            at = T * s + P * tb
                            for c in range(C):
                                ins = mm(ps[:, at:at + P], w[:, c, P * m:P * m + P], xT[:, c, P * tb:P * tb + P],
                                         start=(c == 0), stop=(c == C - 1))
                        if tb:
                            bank_made(ins, ("sgu", L, m))

                xt(1 + 2 * L, 0)
                xt_there(1 + 2 * L, 0)
                shared_gate_up(0)
                xt(1 + 2 * L, 1)
                xt_there(1 + 2 * L, 1)
                pe.wait_ge(S("router_w"), 32 * (L + 1))
                ps = bank_open(pe, ("router", L))
                for tb in range(TB):
                    for c in range(C):
                        ins = mm(ps[:, NE * tb:NE * tb + NE], xT[:, c, P * tb:P * tb + P], rw[:, c, :],
                                 start=(c == 0), stop=(c == C - 1))
                bank_made(ins, ("router", L))
                shared_gate_up(1)
                pe.wait_ge(S("taken"), L + 1)
                pe.wait_ge(S("consts"), 6)
                ps = bank_open(pe, ("pos", L))
                mm(ps[:, 0:NE], before[:], taken[:, 0, :], start=True, stop=True)
                mm(ps[:, NE:2 * NE], ones[:], taken[:, 0, :], start=True, stop=False)
                mm(ps[:, NE:2 * NE], before[:], taken[:, 1, :], start=False, stop=True)
                mm(ps[:, 2 * NE:3 * NE], ones[:], taken[:, 0, :], start=True, stop=False)
                ins = mm(ps[:, 2 * NE:3 * NE], ones[:], taken[:, 1, :], start=False, stop=True)
                bank_made(ins, ("pos", L))
                unit_wait(pe, ("shared", L, 2))
                dw = by_pair(unit(("shared", L, 2)))
                for m in range(2):
                    bank_moved(pe, ("sgu", L, m))
                for tb in range(TB):
                    for h in range(2):
                        ps = bank_open(pe, ("sdn", L, tb, h))
                        for m in range(2):
                            ins = mm(ps[:], hidS[:, m, P * tb:P * tb + P], dw[:, m, HALF * h:HALF * h + HALF],
                                     start=(m == 0), stop=(m == 1))
                        bank_made(ins, ("sdn", L, tb, h))

                def gather(c, ps):
                    for tb in range(TB):
                        for k in range(3):
                            part = xs[k][:, tb, :].rearrange("t (p c) -> t c p", c=C)
                            ins = mm(ps[:, 0:GSLOT], part[:, c, :], pick[:, tb, :],
                                     start=(tb + k == 0), stop=(tb == 1 and k == 2))
                    return ins

                def weights_landed(lp, j, w):
                    if lp.r is None:
                        u, base, _ = loop_unit(L, j, w)
                        pe.wait_ge(S(f"unit_full{u}"), lp.groups(16, 16 * (base + 1)))
                    elif j % 2 == 0 and w != 1:
                        n = 64 if w == 0 else 32
                        pe.wait_ge(lp.sem(weights_of(j, w)), lp.r * (n * NGRP) + lp.groups(n, n))

                def gate_up(lp, pr):
                    ps = lp.open(pe, ("gu", pr))
                    for q in range(2):
                        for w in range(2):
                            weights_landed(lp, 2 * pr + q, w)
                    for c in range(C):
                        for q in range(2):
                            j = 2 * pr + q
                            u = loop_unit(L, j, 0)[0]
                            both = ring[:, u * UNIT:(u + 2) * UNIT].rearrange("p (w c f) -> p c w f", w=2, c=C)
                            ins = mm(ps[SLOTS * q:SLOTS * q + SLOTS, :], xg[:, c, SLOTS * j:SLOTS * j + SLOTS],
                                     both[:, c], start=(c == 0), stop=(c == C - 1))
                    lp.made(ins, ("gu", pr))

                def flip_hidden(lp, pr):
                    ps = lp.open(pe, ("hT", pr))
                    rows = hid[pr].rearrange("s (p m) -> s m p", m=2)
                    for m in range(2):
                        ins = flip(ps[:, P * m:P * m + P], rows[:, m, :], ident[:])
                    lp.made(ins, ("hT", pr))

                def down(lp, pr):
                    lp.moved(pe, ("hT", pr))
                    for q in range(2):
                        weights_landed(lp, 2 * pr + q, 2)
                    for h in range(2):
                        ps = lp.open(pe, ("dn", pr, h))
                        for m in range(2):
                            for q in range(2):
                                wt = loop_weights(L, 2 * pr + q, 2)
                                ins = mm(ps[SLOTS * q:SLOTS * q + SLOTS, :], hidT[pr][:, m, SLOTS * q:SLOTS * q + SLOTS],
                                         wt[:, m, HALF * h:HALF * h + HALF], start=(m == 0), stop=(m == 1))
                        lp.made(ins, ("dn", pr, h))

                def group(lp, last=False):
                    def gathers(lp, cs):
                        for c in cs if not last else ():
                            lp.made(gather(c, lp.open(pe, ("gather", c))), ("gather", c))

                    pe.wait_ge(lp.sem("pick"), lp.count(2, 2, 0))
                    ps = lp.open(pe, "gT")
                    for pr in range(2):
                        for tb in range(TB):
                            ins = flip(ps[:, T * pr + P * tb:T * pr + P * tb + P], pickg[:, tb, P * pr:P * pr + P], ident[:])
                    lp.made(ins, "gT")
                    for b in GATHER_BANKS:
                        per = banks.per[L][b]
                        if lp.r is None:
                            pe.wait_ge(S(f"bank_free{b}"), lp.groups(per, banks.base[L][b]))
                        else:
                            pe.wait_ge(lp.sem(f"free{b}"), lp.count(per, C // 2, 0) + 1)
                    gate_up(lp, 0)
                    gate_up(lp, 1)
                    flip_hidden(lp, 0)
                    if not last:
                        pe.wait_ge(lp.sem("pick"), lp.count(2, 2, 1))
                    gathers(lp, (0, 1))
                    down(lp, 0)
                    flip_hidden(lp, 1)
                    gathers(lp, (2, 3))
                    down(lp, 1)
                    gathers(lp, (4, 5, 6, 7))
                    pe.wait_ge(lp.sem("hot"), lp.count(1, 0, 1))
                    for tb in range(TB):
                        for pr in range(2):
                            if tb == 0:
                                pe.wait_ge(lp.sem("low"), lp.count(2, 0, pr + 1))
                            for h in range(2):
                                key = ("scatter", 2 * tb + h)
                                ps = lp.open(pe, key) if pr == 0 else bank[lp.at(key)[0]]
                                for k in range(3):
                                    ins = mm(ps[:], hot[:, pr, P * tb:P * tb + P],
                                             ys[k][:, pr, HALF * h:HALF * h + HALF],
                                             start=(pr + k == 0), stop=(pr == 1 and k == 2))
                                if pr:
                                    lp.made(ins, key)

                lp = ExpertLoop(L, banks, S, bank)
                pe.wait_ge(S("xs"), 2 * L + 2)
                pe.wait_ge(lp.sem("pick"), 1)
                for c in range(C):
                    bank_made(gather(c, bank_open(pe, ("gather", L, c))), ("gather", L, c))
                run_groups(pe, lp, group)
                pe.wait_ge(S("rounds"), L + 1)
                more = pe.value_load(rounds[0:1, 0:1], min_val=0, max_val=MAXR - 1)
                with pe.If(more > 0):
                    for b in range(8):
                        pe.wait_ge(S(f"bank_free{b}"), banks.end[L][b])
                        pe.sem_inc(S(f"more{L}_free{b}"), 1)
                    with pe.Fori(0, more) as r:
                        lp = ExpertLoop(L, banks, S, bank, r)
                        pe.wait_ge(lp.sem("pick"), lp.count(2, 2, -1))
                        for c in range(C):
                            lp.made(gather(c, lp.open(pe, ("first", c))), ("first", c))
                        run_groups(pe, lp, group, whole=True)
                    for b in range(8):
                        n = NGRP * banks.per[L][b] + (C // 2 if b in GATHER_BANKS else 0)
                        pe.wait_ge(S(f"more{L}_free{b}"), more * n + 1)
                    pe.nop()
                with pe.Else():
                    pe.nop()

        def prog_scalar(act):
            fn = nc.scalar.activation

            def xt(n, k):
                ps = bank_read(act, ("xt", n, k))
                tb, g = divmod(k, 2)
                ins = fn(xT[:, 4 * g:4 * g + 4, P * tb:P * tb + P], ps[:].rearrange("p (c t) -> p c t", c=4), ACT.Copy)
                bank_done(ins, ("xt", n, k))

            def attention(L, heads, first, before=None, after=None):
                for h in range(heads + 2):
                    if before and h < heads:
                        before(h)
                    if h < heads:
                        s = sc[h % 3]
                        act.wait_ge(S("softmax"), first + h + 1)
                        fn(s[:, 0:P], s[:, 0:P], ACT.Exp, bias=mx[:, h % 2, 2:3], accum_out=rs[:, h % 2, 0:1])
                        fn(s[:, P:P + T], s[:, P:P + T], ACT.Exp, bias=mx[:, h % 2, 3:4],
                           accum_out=rs[:, h % 2, 1:2]).then_inc(S("exps"), 1)
                    if 1 <= h <= heads:
                        g = h - 1
                        ps = bank_read(act, ("pt", L, g))
                        ins = fn(pt[g % 2], ps[:, 0:384], ACT.Copy)
                        bank_done(ins, ("pt", L, g))
                    if h >= 2 and h % 2:
                        g = (h - 3) // 2
                        ps = bank_read(act, ("ot", L, g))
                        ins = fn(mixT[:, (4 if L == 0 else 0) + g, :], ps[:, 0:T], ACT.Copy)
                        bank_done(ins, ("ot", L, g))
                    if after and h < heads:
                        after(h)

            with nc.allow_non_contiguous_dma(reason="256 positions, one to a partition"):
                act.dma_start(posi[:], I["positions"][0].rearrange("(a p) -> p a", p=P)).then_inc(S("positions"), 16)
            act.dma_start(lpar[:, 0:LAT], bcast(I["l0_b_in"][1024:1440])).then_inc(S("lpar"), 16)
            act.dma_start(lpar[:, LAT:LAT + QL], bcast(I["l0_q_norm_g"])).then_inc(S("lpar"), 16)
            act.dma_start(lpar[:, LAT + QL:], bcast(I["l0_kv_norm_g"])).then_inc(S("lpar"), 16)
            act.dma_start(rows0[0:8], I["l0_b_in"][0:1024].rearrange("(a b) -> a b", a=8)).then_inc(S("rows0"), 16)
            act.dma_start(mixT[8:12, 3, 0:P], I["l0_conv_b"].rearrange("(a b) -> a b", a=4)).then_inc(S("rows0"), 16)
            act.dma_start(taps0, I["l0_conv_w"]).then_inc(S("rows0"), 16)
            for k in (0, 2):
                xt(0, k)
            with nc.allow_non_contiguous_dma(reason="16 biases, one to a partition"):
                act.dma_start(fbias[:], I["l1_b_in"][3 * D:].rearrange("(p a) -> p a", a=1)).then_inc(S("fbias"), 16)
            act.dma_start(cln[:, 0, :], bcast(I["l0_conv_ln_g"])).then_inc(S("cln"), 16)
            act.dma_start(cln[:, 1, :], bcast(I["l0_conv_ln_b"])).then_inc(S("cln"), 16)
            act.dma_start(rows1[:], I["l1_b_in"][0:2048].rearrange("(a b) -> a b", a=16)).then_inc(S("rows1"), 16)
            ps = bank_read(act, "cols0")
            bank_done(fn(cols[:], ps[:, 0:12 + CC * TAPS], ACT.Copy), "cols0")
            act.wait_ge(S("angles"), 1)
            fn(turn[:], ang, ACT.Sin).then_inc(S("turn"), 1)
            bank_moved(act, "cols0")

            def open_gate(j):
                ps = bank_read(act, ("ag", j))
                fn(uacc[:, j, :], ps[:, T:2 * T], ACT.Sigmoid, bias=cols[:, 4 + j:5 + j]).then_inc(S("gate"), 1)

            def diagonals(k0, k1):
                for k in range(k0, k1):
                    w = 12 + TAPS * PE_CHUNK + k
                    ins = fn(diag[:, k, :], ident[:], ACT.Copy, scale=cols[:, w:w + 1])
                return ins

            bank_read(act, ("lat", 1))
            diagonals(0, EARLY)
            open_gate(0)
            for tb in range(TB):
                ps = bank_read(act, ("latT", tb))
                ins = fn(latT[:, :, P * tb:P * tb + P], ps[:, 0:384].rearrange("p (c t) -> p c t", c=3), ACT.Copy)
                bank_done(ins, ("latT", tb))
            for tb in range(TB):
                for h in range(2):
                    ps = bank_read(act, ("q", tb, h))
                    ins = fn(qrow[:, tb, 4 * h:4 * h + 4, :], ps[:, 0:384].rearrange("p (h d) -> p h d", h=4), ACT.Copy)
                    bank_done(ins, ("q", tb, h))
            for tb in range(TB):
                for h in range(2):
                    ps = bank_read(act, ("kv", tb, h))[:].rearrange("p (h d) -> p h d", h=4)
                    fn(krow[:, tb, 4 * h:4 * h + 4, 0:NOPE], ps[:, :, 0:NOPE], ACT.Copy)
                    ins = fn(V0[:, tb, 256 * h:256 * h + 256].rearrange("p (h d) -> p h d", h=4), ps[:, :, NOPE:], ACT.Copy)
                    bank_done(ins, ("kv", tb, h))
            diagonals(EARLY, TAPS).then_inc(S("diagonals"), 1)
            open_gate(1)
            for tb in range(TB):
                for g in range(2):
                    ps = bank_read(act, ("qT", tb, g))
                    ins = fn(qT0[0:QK, 4 * g:4 * g + 4, P * tb:P * tb + P],
                             ps[0:QK, :].rearrange("p (h t) -> p h t", h=4), ACT.Copy)
                    bank_done(ins, ("qT", tb, g))

            def conv(h):
                if 1 <= h <= 2:
                    open_gate(1 + h)
                if h == POOL_FROM:
                    bank_moved(act, ("ag", POOL_CHUNK))
                steps = H0 - POOL_FROM
                for k in range(max(1, TAPS * (h - POOL_FROM) // steps), TAPS * (h - POOL_FROM + 1) // steps):
                    w = 12 + TAPS * POOL_CHUNK + k
                    if k > 4:
                        act.wait_ge(S("conv_pool"), k - 3)
                    fn(tapped[:, k % 4, :], upad[:, POOL_CHUNK, k:k + T], ACT.Copy, scale=cols[:, w:w + 1])\
                        .then_inc(S("tapped"), 1)

            attention(0, H0, 0, conv)
            ps = bank_read(act, "convT")
            bank_done(fn(uacc[:, PE_CHUNK, :], ps[:, 0:T], ACT.Identity, bias=cols[:, 8 + PE_CHUNK:9 + PE_CHUNK]), "convT")
            for tb in range(TB):
                act.wait_ge(S("u_normed"), tb + 1)
                fn(urow[:, tb, :], urow[:, tb, :], ACT.Silu).then_inc(S("u_act"), 1)
            for tb in range(TB):
                ps = bank_read(act, ("uT", tb))
                ins = fn(mixT[:, 0:CC, P * tb:P * tb + P], ps[:].rearrange("p (c t) -> p c t", c=CC), ACT.Copy)
                bank_done(ins, ("uT", tb))
            for L in range(2):
                if L == 1:
                    for k in range(3):
                        xt(2, k)
                    act.wait_ge(S("forget"), 1)
                    fn(fg[1][0:H1], fg[1][0:H1], ACT.Exp).then_inc(S("forget_act"), 1)
                    act.wait_ge(S("forget"), 2)
                    fn(fg[1][0:H1], fg[1][0:H1], ACT.Ln).then_inc(S("forget_act"), 1)
                    act.wait_ge(S("qkcol"), 1)

                    def queries(b):
                        ps = bank_read(act, ("qk", b))
                        for s in range(2):
                            for o in range(2):
                                r = slice(64 * o, 64 * o + 64)
                                ins = fn(qT[0:HD, 4 * b + 2 * s + o, :], ps[r, T * s:T * s + T], ACT.Identity,
                                         bias=qkcol[r, 1, 2 * b + s:2 * b + s + 1], scale=HD ** -0.5)
                        bank_done(ins, ("qk", b))

                    queries(0)
                    attention(1, H1, H0, after=lambda h: queries(h // 4 + 1) if h % 4 == 0 and h < H1 - 4 else None)
                for tb in range(TB):
                    for k in ((0, 1), (2,))[tb]:
                        xt(1 + 2 * L, k)
                    act.wait_ge(S("ln_done"), 4 * L + tb + 1)
                    fn(xs[0][:, tb, :], xrow[:, tb, :], ACT.Copy).then_inc(S("xs_high"), 1)
                for tb in range(TB):
                    act.wait_ge(S("xs_rest"), 2 * L + tb + 1)
                    fn(xs[1][:, tb, :], rest[tb], ACT.Copy).then_inc(S("xs_mid"), 1)
                ps = bank_read(act, ("router", L))
                bank_done(fn(sco, ps[:, 0:TB * NE].rearrange("p (a e) -> p a e", a=TB), ACT.Sigmoid), ("router", L))
                for m in range(2):
                    ps = bank_read(act, ("sgu", L, m))
                    fn(silS[:, m, :], ps[:, 0:T], ACT.Silu).then_inc(S("silS"), 1)

                def gathered(read, done, key):
                    c = key[-1]
                    ps = read(act, key)
                    done(fn(xg[:, c, :], ps[:, 0:GSLOT], ACT.Copy), key)

                def group(lp, last=False):
                    ps = lp.read(act, "gT")
                    for pr in range(2):
                        ins = fn(gT[:, pr, :], ps[:, T * pr:T * pr + T], ACT.Copy, accum_out=gcol[:, pr:pr + 1])
                    lp.done(ins, "gT")

                    def silu(pr):
                        ps = lp.read(act, ("gu", pr))
                        fn(hid[pr], ps[:, 0:HID], ACT.Silu).then_inc(lp.sem("silu"), 1)

                    def flipped(pr):
                        ps = lp.read(act, ("hT", pr))
                        lp.done(fn(hidT[pr], ps[:, 0:2 * P].rearrange("p (m s) -> p m s", m=2), ACT.Copy), ("hT", pr))

                    def rows(pr):
                        for h in range(2):
                            ps = lp.read(act, ("dn", pr, h))
                            fn(ys[0][:, pr, HALF * h:HALF * h + HALF], ps[:], ACT.Copy, scale=gcol[:, pr:pr + 1])\
                                .then_inc(lp.sem("high"), 1)

                    def middle(pr):
                        for h in range(2):
                            lp.moved(act, ("dn", pr, h))
                        fn(ys[1][:, pr, :], rest[pr], ACT.Copy).then_inc(lp.sem("mid"), 1)

                    def tokens(c):
                        if not last:
                            gathered(lp.read, lp.done, ("gather", c))

                    silu(0)
                    silu(1)
                    flipped(0)
                    tokens(0)
                    rows(0)
                    flipped(1)
                    middle(0)
                    tokens(2)
                    rows(1)
                    tokens(4)
                    middle(1)
                    tokens(6)

                for c in range(0, C, 2):
                    gathered(bank_read, bank_done, ("gather", L, c))
                lp = ExpertLoop(L, banks, S, bank)
                run_groups(act, lp, group)
                act.wait_ge(S("rounds"), L + 1)
                more = act.value_load(rounds[0:1, 0:1], min_val=0, max_val=MAXR - 1)
                with act.If(more > 0):
                    with act.Fori(0, more) as r:
                        lp = ExpertLoop(L, banks, S, bank, r)
                        for c in range(0, C, 2):
                            gathered(lp.read, lp.done, ("first", c))
                        run_groups(act, lp, group, whole=True)
                    act.nop()
                with act.Else():
                    act.nop()

        def prog_vector(dve):
            v = nc.vector
            steps, roots = [0], [0]

            def link(ins):
                steps[0] += 1
                ins.then_inc(S("dve_step"), 1)
                dve.wait_ge(S("dve_step"), steps[0])

            def xt(n, ks):
                for k in ks:
                    ps = bank_read(dve, ("xt", n, k))
                    tb = k // 2
                    ins = v.tensor_copy(xT[:, 4:8, P * tb:P * tb + P], ps[:].rearrange("p (c t) -> p c t", c=4))
                    bank_done(ins, ("xt", n, k))

            def inv_sqrt(dst, src, scale, eps):
                roots[0] += 1
                v.tensor_scalar(dst, src, scale, eps, ALU.mult, ALU.add).then_inc(S("variance"), 1)

            def layer_norm(tb, row, g, b):
                link(v.bn_aggr(mv[:, 2 * tb:2 * tb + 2], st[:, tb, :]))
                inv_sqrt(rstd[:, tb:tb + 1], mv[:, 2 * tb + 1:2 * tb + 2], 1.0, LN_EPS)
                link(v.scalar_tensor_tensor(row, row, mv[:, 2 * tb:2 * tb + 1], par[:, g, :], ALU.subtract, ALU.mult))
                dve.wait_ge(S("inv_std"), roots[0])
                v.scalar_tensor_tensor(xrow[:, tb, :], row, rstd[:, tb:tb + 1], par[:, b, :], ALU.mult, ALU.add)\
                 .then_inc(S("ln_done"), 1)

            def attention(L, heads, first, scale, between=None, after=None):
                for h in range(heads + 1):
                    if h < heads:
                        ps = bank_read(dve, ("score", L, h))
                        s = sc[h % 3]
                        if h >= 3:
                            bank_read(dve, ("pt", L, h - 3))
                        v.tensor_tensor_reduce(s[:, 0:P], ps[:, 0:P], mask[:, P:T], scale, NEG, ALU.add, ALU.max,
                                               mx[:, h % 2, 0:1])
                        ins = v.tensor_tensor_reduce(s[:, P:P + T], ps[:, P:P + T], mask[:], scale, NEG, ALU.add,
                                                     ALU.max, mx[:, h % 2, 1:2])
                        bank_done(ins, ("score", L, h))
                        bank_moved(dve, ("score", L, h))
                        v.tensor_scalar(mx[:, h % 2, 2:4], mx[:, h % 2, 0:2], -1.0, None, ALU.mult)\
                         .then_inc(S("softmax"), 1)
                    if between:
                        between(h)
                    if h >= 1:
                        g = h - 1
                        dve.wait_ge(S("exps"), first + g + 1)
                        link(v.reciprocal(rs[:, g % 2, 2:4], rs[:, g % 2, 0:2]))
                        s = sc[g % 3]
                        v.tensor_scalar(s[:, 0:P], s[:, 0:P], rs[:, g % 2, 2:3], None, ALU.mult)
                        v.tensor_scalar(s[:, P:P + T], s[:, P:P + T], rs[:, g % 2, 3:4], None, ALU.mult)\
                         .then_inc(S("probs"), 1)
                    if after and h < heads:
                        after(h)

            def value(j):
                ps = bank_read(dve, ("ag", j))
                dve.wait_ge(S("gate"), j + 1)
                ins = v.scalar_tensor_tensor(upad[:, j, TAPS - 1:], ps[:, 0:T], cols[:, j:j + 1], uacc[:, j, :],
                                             ALU.add, ALU.mult)
                bank_done(ins, ("ag", j))

            def conv(k0, k1):
                if k0 == 0:
                    bank_moved(dve, ("ag", 1))
                    for j in range(DVE_CHUNKS):
                        w = 12 + TAPS * j
                        v.tensor_scalar(uacc[:, j, :], upad[:, j, 0:T], cols[:, w:w + 1], cols[:, 8 + j:9 + j],
                                        ALU.mult, ALU.add).then_inc(S("tap"), 1)
                    k0 = 1
                with dve.Fori(k0, k1) as k:
                    for j in range(DVE_CHUNKS):
                        w = 12 + TAPS * j
                        dve.wait_ge(S("tap"), k * DVE_CHUNKS + (j + 1 - DVE_CHUNKS))
                        v.scalar_tensor_tensor(uacc[:, j, :], upad[:, j, bass.ds(k, T)], cols[:, bass.ds(k + w, 1)],
                                               uacc[:, j, :], ALU.mult, ALU.add).then_inc(S("tap"), 1)

            dve.wait_ge(S("freq"), 1)
            v.memset(upad[:, :, 0:TAPS - 1], 0.0).then_inc(S("pad"), 1)
            xt(0, (1, 3))
            dve.wait_ge(S("positions"), 16)
            link(v.tensor_copy(posf[:], posi[:]))
            a = ang[:, 0]
            turns = cut(att, 128, TB, ROPE // 2)
            for tb in range(TB):
                ins = v.tensor_scalar(a[:, tb, :], freq[:], posf[:, tb:tb + 1], None, ALU.mult)
            link(ins)
            for s in (1, 0):
                link(v.tensor_scalar(turns, a, 1.0 / (2 * np.pi), 0.25 * s, ALU.mult, ALU.add))
                link(v.tensor_scalar(turns, turns, ROUND, None, ALU.add))
                link(v.tensor_scalar(turns, turns, ROUND, None, ALU.subtract))
                for n, part in enumerate(TWO_PI):
                    link(v.scalar_tensor_tensor(ang[:, s], turns, -part, a if n == 0 else ang[:, s], ALU.mult, ALU.add))
                link(v.tensor_scalar(ang[:, s], ang[:, s], 0.5 * np.pi * s, float(np.pi), ALU.add, ALU.min))
                ins = v.tensor_scalar(ang[:, s], ang[:, s], -float(np.pi), None, ALU.max)
                if s:
                    link(ins)
                else:
                    ins.then_inc(S("angles"), 1)
            dve.wait_ge(S("lpar"), 48)
            for tb in range(TB):
                ps = bank_read(dve, ("lat", tb))
                ins = v.tensor_tensor(lat[:, tb, :], ps[:, 0:LAT], lpar[:, 0:LAT], ALU.add)
                bank_done(ins, ("lat", tb))
                bank_moved(dve, ("lat", tb))
                parts = ((0, QL), (QL, KVL))
                for k, (at, n) in enumerate(parts):
                    x = lat[:, tb, at:at + n]
                    ins = v.tensor_tensor_reduce(cut(att, 1024 + 256 * k, n), x, x, 1.0 / n, 0.0, ALU.mult, ALU.add,
                                                 norm[:, 2 * tb + k:2 * tb + k + 1])
                link(ins)
                both = norm[:, 2 * tb:2 * tb + 2]
                inv_sqrt(both, both, 1.0, RMS_EPS)
                dve.wait_ge(S("inv_std"), roots[0])
                for k, (at, n) in enumerate(parts):
                    x = lat[:, tb, at:at + n]
                    ins = v.scalar_tensor_tensor(x, x, norm[:, 2 * tb + k:2 * tb + k + 1],
                                                 lpar[:, LAT + at:LAT + at + n], ALU.mult, ALU.mult)
                ins.then_inc(S("lat_normed"), 1)
            value(0)
            dve.wait_ge(S("turn"), 1)

            def rotate(x1, x2, o1, o2, heads):
                shape = [P, TB, heads, ROPE // 2]
                s, c = (turn[:, k].unsqueeze(2).to_broadcast(shape) for k in range(2))
                t = [a[:, :, 0:heads, :] for a in rt]
                v.tensor_tensor(t[0], x1, c, ALU.mult)
                v.tensor_tensor(t[1], x2, s, ALU.mult)
                v.tensor_tensor(t[2], x2, c, ALU.mult)
                link(v.tensor_tensor(t[3], x1, s, ALU.mult))
                v.tensor_tensor(o1, t[0], t[1], ALU.subtract)
                return v.tensor_tensor(o2, t[2], t[3], ALU.add)

            kr = lat[:, :, QL + KVL:].unsqueeze(2)
            link(rotate(kr[:, :, :, 0:16], kr[:, :, :, 16:32], kr[:, :, :, 0:16], kr[:, :, :, 16:32], 1))
            for tb in range(TB):
                ins = v.tensor_copy(krow[:, tb, :, NOPE:], lat[:, tb:tb + 1, QL + KVL:].to_broadcast([P, H0, ROPE]))
            link(ins)
            for tb in range(TB):
                for h in range(2):
                    bank_moved(dve, ("q", tb, h))
            qa, qb = qrow[:, :, :, NOPE:NOPE + 16], qrow[:, :, :, NOPE + 16:]
            rotate(qa, qb, qa, qb, H0).then_inc(S("qT_rows"), 1)
            v.memset(rs[:], 0.0).then_inc(S("kT_rows"), 1)
            value(1)
            for tb in range(TB):
                for g in range(2):
                    ps = bank_read(dve, ("kT", tb, g))
                    ins = v.tensor_copy(kT0[0:QK, 4 * g:4 * g + 4, P * tb:P * tb + P],
                                        ps[0:QK, :].rearrange("p (h t) -> p h t", h=4))
                    bank_done(ins, ("kT", tb, g))
            attention(0, H0, 0, QK ** -0.5, lambda h: conv(DVE_CUTS[h], DVE_CUTS[h + 1]),
                      lambda h: value(1 + h) if 1 <= h <= 2 else None)
            dve.wait_ge(S("tap"), TAPS * DVE_CHUNKS)
            v.memset(st[:], 0.0).then_inc(S("conv_dve"), 1)
            dve.wait_ge(S("cln"), 32)
            for tb in range(TB):
                ps = bank_read(dve, ("urow", tb))
                link(v.bn_stats(st[:, tb, 0:6], ps[:]))
                link(v.bn_aggr(mv[:, 2 * tb:2 * tb + 2], st[:, tb, 0:6]))
                inv_sqrt(rstd[:, tb:tb + 1], mv[:, 2 * tb + 1:2 * tb + 2], 1.0, LN_EPS)
                ins = v.scalar_tensor_tensor(urow[:, tb, :], ps[:], mv[:, 2 * tb:2 * tb + 1], cln[:, 0, :],
                                             ALU.subtract, ALU.mult)
                bank_done(ins, ("urow", tb))
                bank_moved(dve, ("urow", tb))
                dve.wait_ge(S("inv_std"), roots[0])
                v.scalar_tensor_tensor(urow[:, tb, :], urow[:, tb, :], rstd[:, tb:tb + 1], cln[:, 1, :],
                                       ALU.mult, ALU.add).then_inc(S("u_normed"), 1)

            for L in range(2):
                if L == 1:
                    xt(2, (3,))
                    ps = bank_read(dve, "cols1")
                    bank_done(v.tensor_copy(qkcol[:, 0, :], ps[:, 0:16]), "cols1")
                    bank_moved(dve, "cols1")
                    v.tensor_copy(qkcol[:, 1, 8:16], qkcol[:, 0, 8:16])
                    v.tensor_scalar(qkcol[:, 1, 0:8], qkcol[:, 0, 0:8], HD ** -0.5, None, ALU.mult).then_inc(S("qkcol"), 1)
                    z, e, one, F, nF = (f[0:H1] for f in fg)
                    ps = bank_read(dve, "forget")
                    dve.wait_ge(S("fbias"), 16)
                    ins = v.tensor_scalar(z, ps[0:H1, 0:T], fbias[:], None, ALU.add)
                    bank_done(ins, "forget")
                    bank_moved(dve, "forget")
                    link(v.memset(one, 1.0))
                    v.scalar_tensor_tensor(e, z, -1.0, z, ALU.mult, ALU.min).then_inc(S("forget"), 1)
                    dve.wait_ge(S("forget_act"), 1)
                    v.tensor_scalar(e, e, 1.0, None, ALU.add).then_inc(S("forget"), 1)
                    dve.wait_ge(S("forget_act"), 2)
                    link(v.scalar_tensor_tensor(z, z, 0.0, e, ALU.min, ALU.subtract))
                    link(v.tensor_tensor_scan(F, one, z, 0.0, ALU.mult, ALU.add))
                    v.tensor_scalar(nF, F, -1.0, None, ALU.mult).then_inc(S("decay"), 1)

                    def keys(b):
                        ps = bank_read(dve, ("qk", 4 + b))
                        for s in range(2):
                            for o in range(2):
                                r = slice(64 * o, 64 * o + 64)
                                n = 2 * (4 + b) + s
                                ins = v.tensor_scalar(kT[0:HD, 4 * b + 2 * s + o, :], ps[r, T * s:T * s + T],
                                                      qkcol[r, 0, n:n + 1], None, ALU.add)
                        bank_done(ins, ("qk", 4 + b))

                    def values(b):
                        ps = bank_read(dve, ("v", b))
                        cs = slice(256 * b, 256 * b + 256)
                        ins = v.tensor_tensor(V1[:, :, cs], ps[:].rearrange("p (t n) -> p t n", t=TB),
                                              vbias[:, cs].unsqueeze(1).to_broadcast([P, TB, 256]), ALU.add)
                        bank_done(ins, ("v", b))

                    def next_heads(h):
                        if h % 4 == 1 and h < H1 - 4:
                            keys(h // 4 + 1)
                        if h % 4 == 3 and h < H1 - 4:
                            values(h // 4 + 1)

                    keys(0)
                    dve.wait_ge(S("vbias"), 16)
                    values(0)
                    dve.wait_ge(S("decay_rows"), 32)
                    attention(1, H1, H0, 1.0, after=next_heads)
                dve.wait_ge(S("scaled"), 4 * L + 4)
                dve.wait_ge(S(f"par{L}"), 48)
                for tb in range(TB):
                    for h in range(2):
                        ps = bank_read(dve, ("mix", L, tb, h))
                        part = xrow[:, tb, HALF * h:HALF * h + HALF]
                        bank_done(v.tensor_tensor(part, part, ps[:], ALU.add), ("mix", L, tb, h))
                        bank_moved(dve, ("mix", L, tb, h))
                        ins = v.bn_stats(st[:, tb, 6 * h:6 * h + 6], part)
                    link(ins)
                    layer_norm(tb, xrow[:, tb, :], 1, 2)
                xt(1 + 2 * L, (3,))
                for tb in range(TB):
                    dve.wait_ge(S("xs_high"), 2 * L + tb + 1)
                    v.tensor_tensor(rest[tb], xrow[:, tb, :], xs[0][:, tb, :], ALU.subtract).then_inc(S("xs_rest"), 1)
                bank_moved(dve, ("router", L))
                dve.wait_ge(S("router_w"), 32 * (L + 1))
                v.memset(gsx[:], SENT)
                v.memset(chx[:, :, NE:], SENT)
                v.memset(want[:], SENT)
                link(v.tensor_tensor(cho, sco, rbias[:].unsqueeze(1).to_broadcast([P, TB, NE]), ALU.add))
                for tb in range(TB):
                    for g in range(NG):
                        ins = v.max(m8[:, tb, g, :], cho[:, tb, GS * g:GS * g + GS])
                link(ins)
                link(v.tensor_tensor(gsx[:, :, 0:NG], m8[:, :, :, 0], m8[:, :, :, 1], ALU.add))
                for tb in range(TB):
                    ins = v.max(top[:, tb, :], gsx[:, tb, 0:NG])
                link(ins)
                link(v.tensor_copy(want[:, :, 0:TOPG], top[:, :, 0:TOPG]))
                for tb in range(TB):
                    ins = v.match_replace(gsr[:, tb, :], want[:, tb, :], gsx[:, tb, :], TAKEN)
                link(ins)
                link(v.tensor_scalar(pen[:], gsr[:, :, 0:NG], TAKEN, NEG, ALU.not_equal, ALU.mult))
                link(v.tensor_tensor(chx[:, :, 0:NE].rearrange("p a (g k) -> p a g k", g=NG),
                                     cho.rearrange("p a (g k) -> p a g k", g=NG),
                                     pen[:].unsqueeze(3).to_broadcast([P, TB, NG, GS]), ALU.add))
                for tb in range(TB):
                    ins = v.max(top[:, tb, :], chx[:, tb, 0:NE])
                link(ins)
                link(v.tensor_copy(want[:, :, 0:TOPK], top[:, :, 0:TOPK]))
                for tb in range(TB):
                    ins = v.match_replace(exr[:, tb, 0:NE + 2], want[:, tb, :], chx[:, tb, 0:NE + 2], TAKEN)
                link(ins)
                v.tensor_scalar(taken, exr[:, :, 0:NE], TAKEN, None, ALU.is_equal).then_inc(S("taken"), 1)
                v.memset(gates[:], 0.0)
                v.memset(posm[:], FAR)
                dve.wait_ge(S("taken"), L + 1)
                link(v.tensor_tensor(cho, sco, taken, ALU.mult))
                link(v.tensor_reduce(norm[:, 0:2], cho, AX.X, ALU.add))
                link(v.reciprocal(norm[:, 2:4], norm[:, 0:2]))
                for tb in range(TB):
                    v.tensor_scalar(gates[:, tb, 0:NE], cho[:, tb, :], norm[:, 2 + tb:3 + tb], SCALE, ALU.mult, ALU.mult)
                link(v.tensor_scalar(exr[:, :, 0:NE], taken, -FAR, FAR, ALU.mult, ALU.add))
                for m in range(2):
                    ps = bank_read(dve, ("sgu", L, m))
                    dve.wait_ge(S("silS"), 2 * L + m + 1)
                    bank_done(v.tensor_tensor(hidS[:, m, :], silS[:, m, :], ps[:, T:2 * T], ALU.mult), ("sgu", L, m))
                ps = bank_read(dve, ("pos", L))
                v.tensor_tensor(posm[:, :, 0:NE], exr[:, :, 0:NE], ps[:, 0:TB * NE].rearrange("p (a e) -> p a e", a=TB), ALU.add)
                ins = v.tensor_reduce(norm[:, 0:1], ps[:, TB * NE:3 * NE], AX.X, ALU.max)
                bank_done(ins, ("pos", L))
                bank_moved(dve, ("pos", L))
                link(v.tensor_scalar(norm[:, 1:2], norm[:, 0:1], float(SLOTS), None, ALU.is_gt))
                link(v.scalar_tensor_tensor(norm[:, 2:3], norm[:, 0:1], 2.0 * SLOTS, norm[:, 1:2], ALU.is_gt, ALU.add))
                v.scalar_tensor_tensor(rounds[:], norm[:, 0:1], 3.0 * SLOTS, norm[:, 2:3], ALU.is_gt, ALU.add)\
                 .then_inc(S("rounds"), 1)

                for tb in range(TB):
                    dve.wait_ge(S("xs_mid"), 2 * L + tb + 1)
                    v.tensor_tensor(xs[2][:, tb, :], rest[tb], xs[1][:, tb, :], ALU.subtract).then_inc(S("xs"), 1)

                def select(lp, g, off):
                    cell = [P, TB, GE, SLOTS]
                    where = posm[:, :, bass.ds(g, GE)] if not isinstance(g, int) else posm[:, :, g:g + GE]
                    gate = gates[:, :, bass.ds(g, GE)] if not isinstance(g, int) else gates[:, :, g:g + GE]
                    grid = iota[:].unsqueeze(1).unsqueeze(1).to_broadcast(cell)
                    v.tensor_tensor(pick.rearrange("p a (j s) -> p a j s", j=GE),
                                    where.unsqueeze(3).to_broadcast(cell), grid, ALU.is_equal).then_inc(lp.sem("pick"), 1)
                    dve.wait_ge(lp.sem("pick"), off)
                    v.tensor_tensor(pickg.rearrange("p a (j s) -> p a j s", j=GE),
                                    pick.rearrange("p a (j s) -> p a j s", j=GE),
                                    gate.unsqueeze(3).to_broadcast(cell), ALU.mult).then_inc(lp.sem("pick"), 1)

                dve.wait_ge(S("consts"), 6)

                def gathered(read, done, key):
                    c = key[-1]
                    ps = read(dve, key)
                    done(v.tensor_copy(xg[:, c, :], ps[:, 0:GSLOT]), key)

                def group(lp, last=False):
                    lp.read(dve, "gT")
                    if not last:
                        select(lp, lp.groups(GE, GE), lp.count(2, 2, 1))

                    def hidden(pr):
                        ps = lp.read(dve, ("gu", pr))
                        dve.wait_ge(lp.sem("silu"), lp.count(GE // 2, 0, pr + 1))
                        lp.done(v.tensor_tensor(hid[pr], hid[pr], ps[:, HID:2 * HID], ALU.mult), ("gu", pr))

                    def rows(pr):
                        for h in range(2):
                            part = slice(HALF * h, HALF * h + HALF)
                            ps = lp.read(dve, ("dn", pr, h))
                            dve.wait_ge(lp.sem("high"), lp.count(4, 0, 2 * pr + h + 1))
                            ins = v.scalar_tensor_tensor(rest[pr][:, part], ps[:], gcol[:, pr:pr + 1],
                                                         ys[0][:, pr, part], ALU.mult, ALU.subtract)
                            lp.done(ins, ("dn", pr, h))

                    def low(pr):
                        dve.wait_ge(lp.sem("mid"), lp.count(2, 0, pr + 1))
                        v.tensor_tensor(ys[2][:, pr, :], rest[pr], ys[1][:, pr, :], ALU.subtract)\
                         .then_inc(lp.sem("low"), 1)

                    def tokens(c):
                        if not last:
                            gathered(lp.read, lp.done, ("gather", c))

                    lp.moved(dve, "gT")
                    v.tensor_scalar(hot, gT, 0.0, None, ALU.not_equal).then_inc(lp.sem("hot"), 1)
                    hidden(0)
                    hidden(1)
                    tokens(1)
                    rows(0)
                    tokens(3)
                    low(0)
                    rows(1)
                    tokens(5)
                    low(1)
                    tokens(7)
                    if not last:
                        for n in range(4):
                            add_rows(lp, n)

                def add_rows(lp, n):
                    tb, h = divmod(n, 2)
                    ps = lp.read(dve, ("scatter", n))
                    part = acc[:, tb, HALF * h:HALF * h + HALF]
                    lp.done(v.tensor_tensor(part, part, ps[:], ALU.add), ("scatter", n))

                def normed(tb):
                    for h in range(2):
                        ins = v.bn_stats(st[:, tb, 6 * h:6 * h + 6], acc[:, tb, HALF * h:HALF * h + HALF])
                    link(ins)
                    layer_norm(tb, acc[:, tb, :], 3, 4)

                def all_read():
                    for b in range(8):
                        dve.wait_ge(S(f"bank_free{b}"), banks.end[L][b])

                lp = ExpertLoop(L, banks, S, bank)
                link(v.memset(st[:], 0.0))
                select(lp, 0, 1)
                for c in range(1, C, 2):
                    gathered(bank_read, bank_done, ("gather", L, c))
                for tb in range(TB):
                    for h in range(2):
                        ps = bank_read(dve, ("sdn", L, tb, h))
                        part = slice(HALF * h, HALF * h + HALF)
                        ins = v.scalar_tensor_tensor(acc[:, tb, part], xrow[:, tb, part], ALPHA, ps[:], ALU.mult, ALU.add)
                        bank_done(ins, ("sdn", L, tb, h))
                for tb in range(TB):
                    for h in range(2):
                        bank_moved(dve, ("sdn", L, tb, h))
                dve.wait_ge(S("rounds"), L + 1)
                more = dve.value_load(rounds[0:1, 0:1], min_val=0, max_val=MAXR - 1)
                run_groups(dve, lp, group)
                dve.wait_ge(S(f"ln2par{L}"), 32)
                first_round, counts = lp, (steps[0], roots[0])
                with dve.If(more > 0):
                    for n in range(4):
                        add_rows(first_round, n)
                    with dve.Fori(0, more) as r:
                        lp = ExpertLoop(L, banks, S, bank, r)
                        v.tensor_scalar(posm[:], posm[:], -float(SLOTS), None, ALU.add).then_inc(lp.sem("round"), 1)
                        dve.wait_ge(lp.sem("round"), r + 1)
                        select(lp, 0, lp.count(2, 2, -1))
                        for c in range(1, C, 2):
                            gathered(lp.read, lp.done, ("first", c))
                        run_groups(dve, lp, group, whole=True)
                    n = NGRP * banks.per[L][GATHER_BANKS[0]] + C // 2
                    dve.wait_ge(S(f"more{L}_free{GATHER_BANKS[0]}"), more * n + 1)
                    v.memset(spare[:], 0.0).then_inc(S(f"more{L}_round"), 1)
                    all_read()
                    for tb in range(TB):
                        normed(tb)
                with dve.Else():
                    steps[0], roots[0] = counts
                    for tb in range(TB):
                        for h in range(2):
                            add_rows(first_round, 2 * tb + h)
                        for h in range(2):
                            first_round.moved(dve, ("scatter", 2 * tb + h))
                        if tb == TB - 1:
                            all_read()
                        normed(tb)

        def prog_gpsimd(pool):
            g = nc.gpsimd

            g.memset(ident[:], 0.0).then_inc(S("ident"), 1)
            pool.wait_ge(S("ident"), 1)
            g.affine_select(out=ident[:], in_=ident[:], compare_op=ALU.not_equal, fill=1.0, base=0,
                            pattern=[[-1, P]], channel_multiplier=1).then_inc(S("ident"), 1)
            g.memset(half[:], -0.5).then_inc(S("half"), 1)
            for k in range(ROPE // 2):
                ins = g.memset(freq[:, k:k + 1], float(FREQ[k]))
            ins.then_inc(S("freq"), 1)
            g.memset(mask[:], 0.0).then_inc(S("consts"), 1)
            g.memset(before[:], 1.0).then_inc(S("consts"), 1)
            g.memset(ones[:], 1.0).then_inc(S("consts"), 1)
            g.iota(iota[:], pattern=[[1, SLOTS]], base=0, channel_multiplier=0,
                   allow_small_or_imprecise_dtypes=True).then_inc(S("consts"), 1)
            pool.wait_ge(S("consts"), 4)
            g.affine_select(out=mask[:, P:T], in_=mask[:, P:T], compare_op=ALU.is_ge, fill=NEG, base=0,
                            pattern=[[-1, P]], channel_multiplier=1).then_inc(S("consts"), 1)
            g.affine_select(out=before[:], in_=before[:], compare_op=ALU.is_gt, fill=0.0, base=0,
                            pattern=[[1, P]], channel_multiplier=-1).then_inc(S("consts"), 1)

            done_roots = [0]

            def power(ap):
                done_roots[0] += 1
                pool.wait_ge(S("variance"), done_roots[0])
                g.tensor_tensor(ap, ap, half[:, 0:ap.shape[-1]], ALU.pow).then_inc(S("inv_std"), 1)

            def params(L, k, name):
                g.dma_start(par[:, k, :], bcast(I[f"l{L}_{name}"]))\
                 .then_inc(S(f"{'par' if k < 3 else 'ln2par'}{L}"), 16)

            def router(L):
                g.dma_start(rw[:], I[f"l{L}_router_w"].rearrange("(p c) n -> p c n", c=C)).then_inc(S("router_w"), 16)
                g.dma_start(rbias[:], bcast(I[f"l{L}_router_bias"])).then_inc(S("router_w"), 16)

            def scale_x(L):
                for k in range(4):
                    bank_read(pool, ("xt", 2 * L, k))
                pool.wait_ge(S(f"par{L}"), 48)
                for tb in range(TB):
                    g.tensor_scalar(xrow[:, tb, :], xrow[:, tb, :], ALPHA, None, ALU.mult).then_inc(S("scaled"), 1)
                    pool.wait_ge(S("scaled"), 4 * L + 2 * tb + 1)
                    g.tensor_tensor(xrow[:, tb, :], xrow[:, tb, :], par[:, 0, :], ALU.add).then_inc(S("scaled"), 1)

            pool.wait_ge(S("half"), 1)
            for tb in range(TB):
                power(norm[:, 2 * tb:2 * tb + 2])
            for k, name in enumerate(("b_out", "ln1_g", "ln1_b")):
                params(0, k, name)
            router(0)
            with nc.allow_non_contiguous_dma(reason="16 forget columns"):
                g.dma_start(wf[:], I["l1_w_in"].rearrange("(p c) n -> p c n", c=C)[:, :, 3 * D:]).then_inc(S("wf"), 16)
            scale_x(0)
            j = POOL_CHUNK
            bank_moved(pool, ("ag", j))
            w = 12 + TAPS * j
            g.tensor_scalar(uacc[:, j, :], upad[:, j, 0:T], cols[:, w:w + 1], cols[:, 8 + j:9 + j],
                            ALU.mult, ALU.add).then_inc(S("conv_pool"), 1)
            for k in range(1, TAPS):
                pool.wait_ge(S("tapped"), k)
                pool.wait_ge(S("conv_pool"), k)
                g.tensor_tensor(uacc[:, j, :], uacc[:, j, :], tapped[:, k % 4, :], ALU.add)\
                 .then_inc(S("conv_pool"), 1)

            pool.wait_ge(S("conv_pool"), TAPS)
            for k, name in ((3, "ln2_g"), (4, "ln2_b")):
                params(0, k, name)
            for _ in range(2):
                for tb in range(TB):
                    power(rstd[:, tb:tb + 1])
            pool.wait_ge(S("ln_done"), 2)
            for k, name in enumerate(("b_out", "ln1_g", "ln1_b")):
                params(1, k, name)
            bank_read(pool, ("router", 0))
            pool.wait_ge(S("taken"), 1)
            router(1)
            for tb in range(TB):
                power(rstd[:, tb:tb + 1])
            pool.wait_ge(S("ln_done"), 4)
            for a in (qT, kT):
                g.memset(a[HD:HD + 2, :, :], 1.0).then_inc(S("unit_rows"), 1)
            g.dma_start(vbias, bcast(I["l1_b_in"][2 * D:3 * D])).then_inc(S("vbias"), 16)
            for k, name in ((3, "ln2_g"), (4, "ln2_b")):
                params(1, k, name)
            pool.wait_ge(S("unit_rows"), 2)
            pool.wait_ge(S("decay"), 1)
            g.dma_start(qT[HD:HD + 1, :, :], fg[3][0:H1]).then_inc(S("decay_rows"), 16)
            g.dma_start(kT[HD + 1:HD + 2, :, :], fg[4][0:H1]).then_inc(S("decay_rows"), 16)
            scale_x(1)
            for _ in range(2):
                for tb in range(TB):
                    power(rstd[:, tb:tb + 1])

        with nc.Block() as block:
            @block.sync
            def _(sp):
                prog_sync(sp)

            @block.tensor
            def _(pe):
                prog_tensor(pe)

            @block.scalar
            def _(act):
                prog_scalar(act)

            @block.vector
            def _(dve):
                prog_vector(dve)

            @block.gpsimd
            def _(pool):
                prog_gpsimd(pool)


def kernel(**inputs):
    import concourse.bacc as bacc
    from concourse.bass_utils import run_bass_kernel_spmd

    nc = bacc.Bacc("TRN2", target_bir_lowering=False, num_devices=1)
    arrays, I = {}, {}
    for name, a in inputs.items():
        a = np.ascontiguousarray(a)
        arrays[f"in_{name}"] = a
        I[name] = nc.dram_tensor(f"in_{name}", a.shape, mybir.dt.from_np(a.dtype), kind="ExternalInput").ap()
    out = nc.dram_tensor("out_0", (1, T, D), F32, kind="ExternalOutput").ap()
    program(nc, I, out)
    return run_bass_kernel_spmd(nc, [arrays], core_ids=[0]).results[0]["out_0"]
```
